# Optimizing a Trainium2 kernel written in Bass

```python
import math
import jax, jax.numpy as jnp
from jax import lax
import numpy as np

D_MODEL = 1024
BATCH = 1
SEQ = 256
DEPTH = 1

HEAD_DIM = 64
FOX_HEADS = 8
MOBA_HEADS = 8
FOX_WIDTH = FOX_HEADS * HEAD_DIM
MOBA_WIDTH = MOBA_HEADS * HEAD_DIM
MIX_WIDTH = FOX_WIDTH + MOBA_WIDTH
IN_WIDTH = 4 * FOX_WIDTH + FOX_HEADS + 4 * MOBA_WIDTH
FOX_Q_BLOCK = 128
MOBA_BLOCK = 256
MOBA_TOPK = 3
MOBA_Q_CHUNK = 16
RMS_EPS = 1e-6

kernel_name = "hybrid_fox_moba_block"

def rms_norm(x, g):
    xf = x.astype(jnp.float32)
    y = xf * lax.rsqrt(jnp.mean(xf * xf, axis=-1, keepdims=True) + RMS_EPS)
    return (y * g.astype(jnp.float32)).astype(x.dtype)

def alibi_slopes(n_heads):
    return jnp.asarray(2.0 ** (-8.0 * np.arange(1, n_heads + 1) / n_heads), dtype=jnp.float32)

def split_heads(t, n_heads):
    b, s, _ = t.shape
    return t.reshape(b, s, n_heads, HEAD_DIM).transpose(0, 2, 1, 3)

def merge_heads(t):
    b, h, s, d = t.shape
    return t.transpose(0, 2, 1, 3).reshape(b, s, h * d)

def fox_attention(q, k, v, log_f):
    S = q.shape[2]
    F = jnp.cumsum(log_f, axis=-1)
    scale = HEAD_DIM ** -0.5
    outs = []
    for start in range(0, S, FOX_Q_BLOCK):
        end = start + FOX_Q_BLOCK
        qb = q[:, :, start:end]
        kb = k[:, :, :end]
        vb = v[:, :, :end]
        logits = jnp.einsum('bhtd,bhsd->bhts', qb, kb, preferred_element_type=jnp.float32) * scale
        logits = logits + F[:, :, start:end, None] - F[:, :, None, :end]
        t_pos = jnp.arange(start, end)[:, None]
        s_pos = jnp.arange(end)[None, :]
        logits = jnp.where(s_pos <= t_pos, logits, -jnp.inf)
        p = jax.nn.softmax(logits, axis=-1)
        outs.append(jnp.einsum('bhts,bhsd->bhtd', p.astype(v.dtype), vb))
    return jnp.concatenate(outs, axis=2)

def moba_attention(q, k, v, slopes):
    B, H, S, d = q.shape
    nb = -(-S // MOBA_BLOCK)
    pad = nb * MOBA_BLOCK - S
    kp = jnp.pad(k, ((0, 0), (0, 0), (0, pad), (0, 0)))
    vp = jnp.pad(v, ((0, 0), (0, 0), (0, pad), (0, 0)))
    kblk = kp.reshape(B, H, nb, MOBA_BLOCK, d)
    vblk = vp.reshape(B, H, nb, MOBA_BLOCK, d)
    kmean = jnp.mean(kblk.astype(jnp.float32), axis=3)
    n_sel = min(MOBA_TOPK, nb - 1)
    scale = HEAD_DIM ** -0.5
    n_chunks = S // MOBA_Q_CHUNK
    b_idx = jnp.arange(B)[:, None, None, None]
    h_idx = jnp.arange(H)[None, :, None, None]
    blk_ids = jnp.arange(nb)
    in_blk = jnp.arange(MOBA_BLOCK)

    def chunk_fn(c):
        start = c * MOBA_Q_CHUNK
        qc = lax.dynamic_slice_in_dim(q, start, MOBA_Q_CHUNK, axis=2)
        t_pos = start + jnp.arange(MOBA_Q_CHUNK)
        qblk = start // MOBA_BLOCK
        own_start = qblk * MOBA_BLOCK
        k_own = lax.dynamic_slice_in_dim(kp, own_start, MOBA_BLOCK, axis=2)
        v_own = lax.dynamic_slice_in_dim(vp, own_start, MOBA_BLOCK, axis=2)
        s_own = own_start + in_blk
        dist_own = (t_pos[:, None] - s_own[None, :]).astype(jnp.float32)
        lg_own = jnp.einsum('bhqd,bhkd->bhqk', qc, k_own, preferred_element_type=jnp.float32) * scale
        lg_own = lg_own - slopes[:, None, None] * dist_own
        lg_own = jnp.where(s_own[None, :] <= t_pos[:, None], lg_own, -jnp.inf)
        if n_sel == 0:
            p_own = jax.nn.softmax(lg_own, axis=-1)
            return jnp.einsum('bhqk,bhkd->bhqd', p_own.astype(v.dtype), v_own)
        gate = jnp.einsum('bhqd,bhnd->bhqn', qc.astype(jnp.float32), kmean)
        gate = jnp.where(blk_ids < qblk, gate, -jnp.inf)
        _, sel = lax.top_k(gate, n_sel)
        sel_valid = sel < qblk
        k_sel = kblk[b_idx, h_idx, sel]
        v_sel = vblk[b_idx, h_idx, sel]
        s_sel = sel[..., None] * MOBA_BLOCK + in_blk
        dist_sel = (t_pos[None, None, :, None, None] - s_sel).astype(jnp.float32)
        lg_sel = jnp.einsum('bhqd,bhqnkd->bhqnk', qc, k_sel, preferred_element_type=jnp.float32) * scale
        lg_sel = lg_sel - slopes[None, :, None, None, None] * dist_sel
        lg_sel = jnp.where(sel_valid[..., None], lg_sel, -jnp.inf)
        lg_sel = lg_sel.reshape(B, H, MOBA_Q_CHUNK, n_sel * MOBA_BLOCK)
        p = jax.nn.softmax(jnp.concatenate([lg_sel, lg_own], axis=-1), axis=-1).astype(v.dtype)
        p_sel = p[..., :n_sel * MOBA_BLOCK].reshape(B, H, MOBA_Q_CHUNK, n_sel, MOBA_BLOCK)
        p_own = p[..., n_sel * MOBA_BLOCK:]
        return (jnp.einsum('bhqnk,bhqnkd->bhqd', p_sel, v_sel)
                + jnp.einsum('bhqk,bhkd->bhqd', p_own, v_own))

    outs = lax.map(chunk_fn, jnp.arange(n_chunks))
    return outs.transpose(1, 2, 0, 3, 4).reshape(B, H, S, d)

def setup_inputs(seed: int = 0) -> dict:
    key = jax.random.key(seed)
    kx, k1, k2, k3, k4, k5 = jax.random.split(key, 6)
    x = jax.random.normal(kx, (BATCH, SEQ, D_MODEL), jnp.float32)
    norm_pre_g = 1.0 + 0.02 * jax.random.normal(k1, (DEPTH, D_MODEL), jnp.float32)
    w_in = jax.random.normal(k2, (DEPTH, D_MODEL, IN_WIDTH), jnp.float32) * D_MODEL ** -0.5
    fox_forget_b = jax.random.uniform(k3, (DEPTH, FOX_HEADS), jnp.float32, minval=1.0, maxval=5.0)
    w_out = jax.random.normal(k4, (DEPTH, MIX_WIDTH, D_MODEL), jnp.float32) * MIX_WIDTH ** -0.5
    norm_post_g = 1.0 + 0.02 * jax.random.normal(k5, (DEPTH, D_MODEL), jnp.float32)
    return {"x": x, "norm_pre_g": norm_pre_g, "w_in": w_in, "fox_forget_b": fox_forget_b,
            "w_out": w_out, "norm_post_g": norm_post_g}

def reference(x, norm_pre_g, w_in, fox_forget_b, w_out, norm_post_g):
    sizes = [FOX_WIDTH] * 4 + [FOX_HEADS] + [MOBA_WIDTH] * 4
    offsets = [int(o) for o in np.cumsum(sizes)[:-1]]
    slopes = alibi_slopes(MOBA_HEADS)
    for layer in range(DEPTH):
        h = rms_norm(x, norm_pre_g[layer])
        proj = jnp.einsum('bsd,de->bse', h, w_in[layer])
        q_a, k_a, v_a, g_a, f_a, q_b, k_b, v_b, g_b = jnp.split(proj, offsets, axis=-1)
        log_f = jax.nn.log_sigmoid((f_a + fox_forget_b[layer]).astype(jnp.float32))
        y_a = fox_attention(split_heads(q_a, FOX_HEADS), split_heads(k_a, FOX_HEADS),
                            split_heads(v_a, FOX_HEADS), log_f.transpose(0, 2, 1))
        y_a = merge_heads(y_a) * jax.nn.silu(g_a)
        y_b = moba_attention(split_heads(q_b, MOBA_HEADS), split_heads(k_b, MOBA_HEADS),
                             split_heads(v_b, MOBA_HEADS), slopes)
        y_b = merge_heads(y_b) * jax.nn.silu(g_b)
        y = jnp.einsum('bse,ed->bsd', jnp.concatenate([y_a, y_b], axis=-1), w_out[layer])
        x = x + rms_norm(y, norm_post_g[layer])
    return x


_drawn_inputs = setup_inputs


def setup_inputs(seed=0):
    import zlib

    import numpy as np

    out = dict(_drawn_inputs(seed))
    spreads = {}
    factors = {}
    for name, (base, spread) in spreads.items():
        noise = np.random.default_rng([zlib.crc32(name.encode()), seed]).standard_normal(out[name].shape)
        drawn = base * np.exp(spread * noise) if base else spread * noise
        out[name] = __import__('jax').numpy.asarray(drawn.astype(out[name].dtype))
    for name, factor in factors.items():
        out[name] = (out[name] * factor).astype(out[name].dtype)
    return out
```

```python
from contextlib import ExitStack

import concourse.bass as bass
from concourse import mybir

F32 = mybir.dt.float32
F32R = mybir.dt.float32r
ALU = mybir.AluOpType
ACT = mybir.ActivationFunctionType
AX_X = mybir.AxisListType.X

P = 128
SEQ = 256
D_MODEL = 1024
HEAD_DIM = 64
HEADS = 8
KT = D_MODEL // P
TT = SEQ // P
PAIRS = 2 * HEADS // 2
FOX_PAIRS = HEADS // 2
HALF = D_MODEL // 2
UNIT = 1024
V_UNITS, G_UNITS, QK_UNITS = 8, PAIRS, 2 * PAIRS
UNITS = V_UNITS + G_UNITS + QK_UNITS
QK_0 = V_UNITS + G_UNITS
QK_0 = V_UNITS + G_UNITS
QK_0 = V_UNITS + G_UNITS
QK_0 = V_UNITS + G_UNITS
QK_0 = V_UNITS + G_UNITS
QK_0 = V_UNITS + G_UNITS
QK_0 = V_UNITS + G_UNITS
RING = 4
OUT_OWN = 4
EPS = 1e-6
SCALE = HEAD_DIM ** -0.5
MASKED = -1e32
PARTS = ("hi", "lo")
X_LOADS = 4
N_CONST = 5
PARTS = ("hi", "lo")
X_LOADS = 4
N_CONST = 5
PARTS = ("hi", "lo")
X_LOADS = 4
N_CONST = 5
PARTS = ("hi", "lo")
X_LOADS = 4
N_CONST = 5
PARTS = ("hi", "lo")
X_LOADS = 4
N_CONST = 5
PARTS = ("hi", "lo")
X_LOADS = 4
N_CONST = 5
PARTS = ("hi", "lo")
X_LOADS = 4
N_CONST = 5
PASSES = ((0, 0), (0, 1), (1, 0))
NB = P + SEQ


def hybrid_layer(nc, xt, x, g_pre, w_units, w_f, f_bias, w_out, g_post, out):
    ctx = ExitStack()

    def sb(name, shape, dt=F32):
        return ctx.enter_context(nc.sbuf_tensor(name, shape, dt))

    def sem(name):
        return ctx.enter_context(nc.semaphore(name))

    with ctx:
        x_t = sb("x_t", [P, KT, SEQ])
        xg = [sb(f"xg_{n}", [P, KT, SEQ], F32R) for n in PARTS]
        h32 = sb("h32", [P, KT, SEQ])
        h = [sb(f"h_{n}", [P, KT, SEQ], F32R) for n in PARTS]
        squares = sb("squares", [P, KT, SEQ])
        gpre_col = sb("gpre_col", [P, KT])
        gpost_row = sb("gpost_row", [P, D_MODEL])
        wf = sb("wf", [P, KT, HEADS])
        wfg = sb("wfg", [P, KT, HEADS])
        fb_col = sb("fb_col", [HEADS, 1])
        raw = sb("raw", [P, RING, UNIT])
        w = [sb(f"w_{n}", [P, RING, UNIT], F32R) for n in PARTS]
        raw_out = sb("raw_out", [P, UNIT])
        wo = [sb(f"wo_{n}", [P, OUT_OWN, D_MODEL], F32R) for n in PARTS]
        v = sb("v", [P, 2 * TT, D_MODEL], F32R)
        v_pair = sb("v_pair", [P, 2, 2 * TT, P], F32R)
        q = [sb(f"q_{n}", [P, SEQ], F32R) for n in PARTS]
        k = [sb(f"k_{n}", [P, 2, SEQ], F32R) for n in PARTS]
        bias = sb("bias", [P, 2, NB])
        logits = sb("logits", [P, 2, NB])
        probs = sb("probs", [P, 2, NB])
        p_t0 = [sb(f"p_t0_{n}", [P, 2, SEQ], F32R) for n in PARTS]
        p_t1 = [sb(f"p_t1_{n}", [P, 2, P], F32R) for n in PARTS]
        y32 = sb("y32", [P, SEQ])
        ident = sb("ident", [P, P])
        ones = sb("ones", [P, P])
        causal = sb("causal", [P, NB])
        dist = sb("dist", [P, NB])
        slope_col = sb("slope_col", [P, HEADS])
        diag = sb("diag", [P, TT, P])
        rrow = sb("rrow", [P, SEQ])
        ms = sb("ms", [P, TT])
        root = sb("root", [P, TT])
        rstd = sb("rstd", [P, TT])
        newton = sb("newton", [P, 2, TT])
        mx = sb("mx", [P, 4])
        neg_max = sb("neg_max", [P, 4])
        row_sum = sb("row_sum", [P, 4])
        row_inv = sb("row_inv", [P, 4])
        out_sq = sb("out_sq", [P, TT, 2])
        gate = h32
        y = xg
        decay = squares
        x_nat = x_t[:, :, :].rearrange("p a b -> p (a b)").rearrange("p (t d) -> p t d", t=TT)
        fz = logits[0:HEADS, :, :].rearrange("p a n -> p (a n)").rearrange("p (a n) -> p a n", n=SEQ)
        ones_row = probs[0:HEADS, 0, 0:SEQ]
        f_neg = probs[0:HEADS, 1, 0:SEQ]
        junk = bias[:, :, :].rearrange("p a n -> p (a n)")[:, 0:HALF]
        decay_dram = nc.dram_tensor("decay_rows_scratch", (HEADS, SEQ), F32, kind="Internal").ap()

        bank = [ctx.enter_context(nc.psum_tensor(f"bank{b}", [P, HALF], F32)) for b in range(8)]
        v_banks = [[bank[2], bank[3]], [bank[4], bank[5]]]
        ssq_ps, rrow_ps, f_ps = bank[6], bank[1], bank[7]
        s0_ps = bank[2][:, 0:2 * P].rearrange("p (a n) -> p a n", a=2)
        s1_ps = bank[3][:, :].rearrange("p (a n) -> p a n", a=2)
        pt0_ps = bank[4][:, :].rearrange("p (a n) -> p a n", a=2)
        pt1_ps = bank[5][:, 0:2 * P].rearrange("p (a n) -> p a n", a=2)
        pv_ps = bank[6][:, :].rearrange("p (a n) -> p a n", a=2)
        out_groups = [(0, 0, bank[7]), (0, 1, bank[0]), (1, 0, bank[1]), (1, 1, bank[2])]

        s_small_in = sem("small_in")
        s_x_in = [sem(f"x_in{c}") for c in range(X_LOADS)]
        s_gpost_in, s_xnat_in = sem("gpost_in"), sem("x_nat_in")
        s_raw_in = [sem(f"raw_in{s}") for s in range(RING)]
        s_raw_out_in = sem("raw_out_in")
        s_vpair_in = [sem(f"v_pair_in{s}") for s in range(2)]
        s_hi, s_lo = sem("unit_hi"), sem("unit_lo")
        s_used = sem("unit_used")
        s_ohi, s_olo = sem("out_unit_hi"), sem("out_unit_lo")
        s_pool, s_dve = sem("pool_chain"), sem("dve_chain")
        s_const = sem("constants")
        s_xghi, s_xglo = sem("xg_hi"), sem("xg_lo")
        s_wfg, s_f = sem("wfg_ready"), sem("f_ready")
        s_sq, s_sqsum, s_ssq = sem("squares_done"), sem("square_sums"), sem("ssq_ready")
        s_ms, s_root, s_rstd = sem("mean_square"), sem("root_ready"), sem("rstd_ready")
        s_diag, s_rbc, s_rrow = sem("diag_ready"), sem("rstd_broadcast"), sem("rrow_ready")
        s_fabs, s_fexp, s_fln = sem("f_abs"), sem("f_exp"), sem("f_ln")
        s_decay, s_decay_st, s_decay_in = sem("decay_rows"), sem("decay_stored"), sem("decay_in")
        s_h32, s_hhi, s_hlo = sem("h32_ready"), sem("h_hi"), sem("h_lo")
        s_vhi, s_vlo = sem("v_hi"), sem("v_lo")
        s_gate = sem("gate_ready")
        s_qhi, s_qlo = sem("q_hi"), sem("q_lo")
        s_khi, s_klo = sem("k_hi"), sem("k_lo")
        s_qk = sem("scores_ready")
        s_bias = sem("bias_ready")
        s_logits = sem("logits_ready")
        s_nmax = sem("neg_max_ready")
        s_exp = sem("exp_done")
        s_inv, s_norm = sem("row_inv_ready"), sem("probs_normed")
        s_pt = sem("probs_transposed")
        s_pthi, s_ptlo = sem("pt_hi"), sem("pt_lo")
        s_pv = sem("pv_ready")
        s_y, s_yhi, s_ylo = sem("y_ready"), sem("y_hi"), sem("y_lo")
        s_group = sem("out_group")
        s_osq, s_oms, s_oroot = sem("out_squares"), sem("out_mean_square"), sem("out_root")
        s_fin, s_stored = sem("fin_ready"), sem("stored")

        block = ctx.enter_context(nc.Block())

        @block.sync
        def _(sp):
            n = KT // X_LOADS
            for c in range(X_LOADS):
                sp.dma_start(x_t[:, n * c:n * c + n, :], xt[:, n * c:n * c + n, :]).then_inc(s_x_in[c], 16)
            for s in range(RING):
                sp.dma_start(raw[:, s, :], w_units[s]).then_inc(s_raw_in[s], 16)

            def load_unit(r, s):
                sp.wait_ge(s_lo, r * RING + s + 1 - RING)
                sp.dma_start(raw[:, s, :], w_units[r * RING + s]).then_inc(s_raw_in[s], 16)

            for s in range(RING):
                load_unit(1, s)
            for u in range(V_UNITS, QK_0 + RING):
                load_unit(u // RING, u % RING)
                j = (u - V_UNITS - 3) // 2
                if u % 2 and 0 <= j < OUT_OWN:
                    if j:
                        sp.wait_ge(s_olo, j)
                    sp.dma_start(raw_out[:, :], w_out[j]).then_inc(s_raw_out_in, 16)
            sp.dma_start(gpost_row[:, :], g_post[0:1, :].to_broadcast((P, D_MODEL))).then_inc(s_gpost_in, 16)
            with sp.Fori(QK_0 // RING + 1, UNITS // RING) as r:
                for s in range(RING):
                    load_unit(r, s)
            for s in range(RING):
                sp.wait_ge(s_lo, UNITS + s + 1 - RING)
                sp.dma_start(raw[:, s, :], w_out[OUT_OWN + s]).then_inc(s_raw_in[s], 16)
            sp.wait_ge(s_h32, KT)
            sp.dma_start(x_nat, x).then_inc(s_xnat_in, 16)
            for n, (t, c, _) in enumerate(out_groups):
                sp.wait_ge(s_fin, n + 1)
                sp.dma_start(out[t, :, c * HALF:(c + 1) * HALF],
                             x_nat[:, t, c * HALF:(c + 1) * HALF]).then_inc(s_stored, 16)
            sp.wait_ge(s_stored, 16 * len(out_groups))

        @block.gpsimd
        def _(pool):
            done = [0]

            def link(ins):
                done[0] += 1
                ins.then_inc(s_pool, 1)
                pool.wait_ge(s_pool, done[0])

            link(pool.memset(ident[:, :], 0.0))
            pool.affine_select(out=ident[:, :], in_=ident[:, :], compare_op=ALU.not_equal, fill=1.0,
                               base=0, pattern=[[-1, P]], channel_multiplier=1).then_inc(s_const, 1)
            pool.memset(ones[:, :], 1.0).then_inc(s_const, 1)
            for n in range(2):
                pool.memset(k[n][:, :, :].bitcast(F32), 0.0).then_inc(s_const, 1)
            pool.memset(ones_row, 1.0).then_inc(s_const, 1)
            pool.memset(causal[:, :], 0.0).then_inc(s_pool, 1)
            pool.iota(dist[:, 0:P], pattern=[[1, P]], base=0, channel_multiplier=-1,
                      allow_small_or_imprecise_dtypes=True).then_inc(s_pool, 1)
            pool.iota(dist[:, P:NB], pattern=[[1, SEQ]], base=-P, channel_multiplier=-1,
                      allow_small_or_imprecise_dtypes=True).then_inc(s_pool, 1)
            for n in range(HEADS):
                pool.memset(slope_col[:, n:n + 1], 2.0 ** (-8.0 * (n + 1) / HEADS) / SCALE).then_inc(s_pool, 1)
            done[0] += 3 + HEADS
            pool.wait_ge(s_pool, done[0])
            for m in (causal, dist):
                for lo, hi, base in ((0, P, 0), (P, NB, P)):
                    pool.affine_select(out=m[:, lo:hi], in_=m[:, lo:hi], compare_op=ALU.is_ge, fill=MASKED,
                                       base=base, pattern=[[-1, hi - lo]], channel_multiplier=1).then_inc(s_pool, 1)
                    done[0] += 1

            pool.wait_ge(s_sq, X_LOADS)
            n = KT // 2
            while n > 1:
                link(pool.tensor_tensor(squares[:, 0:n, :], squares[:, 0:n, :], squares[:, n:2 * n, :], ALU.add))
                n //= 2
            pool.tensor_tensor(squares[:, 0, :], squares[:, 0, :], squares[:, 1, :], ALU.add).then_inc(s_sqsum, 1)

            with pool.Fori(0, OUT_OWN) as j:
                pool.wait_ge(s_ohi, j + 1)
                pool.tensor_tensor(wo[1][:, bass.ds(j, 1), :], raw_out[:, :].unsqueeze(1),
                                   wo[0][:, bass.ds(j, 1), :].bitcast(F32), ALU.subtract).then_inc(s_olo, 1)

            def fox_bias(i):
                for lo, hi in ((0, P), (P, NB)):
                    last = pool.tensor_tensor(bias[:, :, lo:hi], decay[:, bass.ds(2 * i, 2), 0:hi - lo],
                                              causal[:, lo:hi].unsqueeze(1).to_broadcast((P, 2, hi - lo)), ALU.add)
                    if lo == 0:
                        last.then_inc(s_bias, 1)
                last.then_inc(s_bias, 1)

            def moba_bias(i):
                for lo, hi in ((0, P), (P, NB)):
                    pool.tensor_tensor(bias[:, :, lo:hi],
                                       dist[:, lo:hi].unsqueeze(1).to_broadcast((P, 2, hi - lo)),
                                       slope_col[:, bass.ds(2 * i - HEADS, 2)].unsqueeze(2).to_broadcast((P, 2, hi - lo)),
                                       ALU.mult).then_inc(s_bias, 1)

            def norm_probs(i):
                pool.wait_ge(s_inv, i + 1)
                for t, (lo, hi) in enumerate(((0, P), (P, NB))):
                    pool.tensor_tensor(probs[:, :, lo:hi], probs[:, :, lo:hi],
                                       row_inv[:, t::2].unsqueeze(2).to_broadcast((P, 2, hi - lo)),
                                       ALU.mult).then_inc(s_norm, 1)

            def y_low(i):
                pool.wait_ge(s_yhi, i + 1)
                pool.tensor_tensor(y[1][:, bass.ds(i, 1), :], y32[:, :].unsqueeze(1),
                                   y[0][:, bass.ds(i, 1), :].bitcast(F32), ALU.subtract).then_inc(s_ylo, 1)

            pool.wait_ge(s_pool, done[0])
            pool.wait_ge(s_decay_in, 16)
            fox_bias(0)
            pool.wait_ge(s_logits, 4)
            fox_bias(1)
            norm_probs(0)
            with pool.Fori(2, FOX_PAIRS) as i:
                pool.wait_ge(s_logits, 4 * i)
                fox_bias(i)
                norm_probs(i - 1)
                y_low(i - 2)
            with pool.Fori(FOX_PAIRS, PAIRS) as i:
                pool.wait_ge(s_logits, 4 * i)
                moba_bias(i)
                norm_probs(i - 1)
                y_low(i - 2)
            norm_probs(PAIRS - 1)
            y_low(PAIRS - 2)
            y_low(PAIRS - 1)

        @block.scalar
        def _(act):
            act.dma_start(gpre_col[:, :], g_pre).then_inc(s_small_in, 16)
            act.dma_start(wf[:, :, :], w_f).then_inc(s_small_in, 16)
            act.dma_start(fb_col[:, :], f_bias).then_inc(s_small_in, 16)

            def unit_high(s, n, used=None):
                act.wait_ge(s_raw_in[s], n)
                if used is not None:
                    act.wait_ge(s_used, used)
                nc.scalar.activation(w[0][:, s, :], raw[:, s, :], ACT.Copy).then_inc(s_hi, 1)

            def out_unit_high(j):
                act.wait_ge(s_raw_out_in, 16 * (j + 1))
                nc.scalar.activation(wo[0][:, bass.ds(j, 1), :], raw_out[:, :].unsqueeze(1), ACT.Copy).then_inc(s_ohi, 1)

            unit_high(0, 16)
            unit_high(1, 16)
            n = KT // X_LOADS
            for c in range(X_LOADS):
                act.wait_ge(s_x_in[c], 16)
                nc.scalar.activation(squares[:, n * c:n * c + n, :], x_t[:, n * c:n * c + n, :],
                                     ACT.Square).then_inc(s_sq, 1)
            unit_high(2, 16)
            unit_high(3, 16)
            act.wait_ge(s_ms, 1)
            nc.scalar.activation(root[:, :], ms[:, :], ACT.Sqrt).then_inc(s_root, 1)
            unit_high(0, 32, 1)
            unit_high(1, 32, 2)

            def value_high(c):
                act.wait_ge(s_used, 4 * c + 4)
                act.wait_ge(s_rstd, 1)
                for t in range(TT):
                    nc.scalar.activation(v[:, t, c * HALF:(c + 1) * HALF], v_banks[c][t][:, :], ACT.Copy,
                                         scale=rstd[:, t:t + 1]).then_inc(s_vhi, 1)

            value_high(0)
            for c in range(2):
                act.wait_ge(s_h32, (c + 1) * KT // 2)
                nc.scalar.activation(h[0][:, c * KT // 2:(c + 1) * KT // 2, :],
                                     h32[:, c * KT // 2:(c + 1) * KT // 2, :], ACT.Copy).then_inc(s_hhi, 1)
            unit_high(2, 32, 3)
            unit_high(3, 32, 4)
            act.wait_ge(s_fabs, 1)
            nc.scalar.activation(fz[:, 1, :], fz[:, 1, :], ACT.Exp, scale=-1.0).then_inc(s_fexp, 1)
            act.wait_ge(s_fexp, 1)
            nc.scalar.activation(fz[:, 2, :], fz[:, 1, :], ACT.Ln, bias=1.0).then_inc(s_fln, 1)
            unit_high(0, 48, 5)
            unit_high(1, 48, 6)
            value_high(1)
            act.wait_ge(s_decay, 1)
            act.dma_start(decay_dram, fz[:, 0, :]).then_inc(s_decay_st, 16)
            act.wait_ge(s_decay_st, 16)
            act.dma_start(decay[:, :, :], decay_dram.partition_broadcast(P)).then_inc(s_decay_in, 16)

            with act.Fori(V_UNITS // RING, QK_0 // RING) as r:
                for s in range(RING):
                    ahead = (s + 2) % RING
                    unit_high(ahead, 16 * (r + 1 + (s + 2) // RING), r * RING + s - 1)
                    if s % 2:
                        out_unit_high(r * 2 - V_UNITS // 2 + s // 2)
                    act.wait_ge(s_used, r * RING + s + 1)
                    nc.scalar.activation(gate[:, bass.ds(r * RING + s - V_UNITS, 1), :],
                                         bank[s % 2][:, 0:SEQ].unsqueeze(1), ACT.Silu).then_inc(s_gate, 1)

            def fetch_values(i, b):
                act.dma_start(v_pair[:, b, :, :].bitcast(F32), v[:, :, bass.ds(i * P, P)].bitcast(F32)).then_inc(s_vpair_in[b], 16)

            def probs_high(i):
                act.wait_ge(s_pt, i + 1)
                nc.scalar.activation(p_t0[0][:, :, :], pt0_ps, ACT.Copy).then_inc(s_pthi, 1)
                nc.scalar.activation(p_t1[0][:, :, :], pt1_ps, ACT.Copy).then_inc(s_pthi, 1)

            def exps(i):
                for a in range(2):
                    act.wait_ge(s_nmax, 2 * i + a + 1)
                    for t, (lo, hi) in enumerate(((0, P), (P, NB))):
                        c = 2 * a + t
                        nc.scalar.activation(probs[:, a, lo:hi], logits[:, a, lo:hi], ACT.Exp,
                                             bias=neg_max[:, c:c + 1], scale=SCALE,
                                             accum_out=row_sum[:, c:c + 1]).then_inc(s_exp, 1)

            def y_high(i):
                act.wait_ge(s_y, 2 * i + 2)
                nc.scalar.activation(y[0][:, bass.ds(i, 1), :], y32[:, :].unsqueeze(1), ACT.Copy).then_inc(s_yhi, 1)

            def query_high(i):
                act.wait_ge(s_used, QK_0 + 1 + 2 * i)
                nc.scalar.activation(q[0][:, :], bank[0][:, 0:SEQ], ACT.Copy).then_inc(s_qhi, 1)

            def key_high(i):
                act.wait_ge(s_used, QK_0 + 2 + 2 * i)
                for a in range(2):
                    rows = slice(a * HEAD_DIM, (a + 1) * HEAD_DIM)
                    nc.scalar.activation(k[0][rows, a, :], bank[1][rows, 0:SEQ], ACT.Copy).then_inc(s_khi, 1)

            def attend(i, b, n, first=0, fresh=False):
                if i is not None and first != 1:
                    if first == 0 and not fresh:
                        act.wait_ge(s_pv, i - 2)
                    fetch_values(i - 1, 1 - b)
                if first == 0:
                    probs_high(i - 2)
                if first != 1:
                    act.wait_ge(s_qk, i)
                query_high(i)
                if first != 1:
                    exps(i - 1)
                unit_high((2 * b + 2) % RING, n, 2 * i + QK_0 - 1)
                key_high(i)
                if first == 0:
                    y_high(i - 2)
                unit_high((2 * b + 3) % RING, n, 2 * i + QK_0)

            act.wait_ge(s_const, N_CONST)
            attend(0, 0, 16 * (QK_0 // RING + 1), first=1)
            act.wait_ge(s_vlo, 4)
            attend(1, 1, 16 * (QK_0 // RING + 2), first=2)
            attend(2, 0, 16 * (QK_0 // RING + 2), fresh=True)
            attend(3, 1, 16 * (QK_0 // RING + 3))
            with act.Fori(2, PAIRS // 2) as it:
                for b in range(2):
                    attend(2 * it + b, b, 16 * (it + QK_0 // RING + 1 + b))
            act.wait_ge(s_pv, PAIRS - 2)
            fetch_values(PAIRS - 1, 1)
            probs_high(PAIRS - 2)
            unit_high(2, 16 * (UNITS // RING + 1), UNITS - 1)
            exps(PAIRS - 1)
            unit_high(3, 16 * (UNITS // RING + 1), UNITS)
            y_high(PAIRS - 2)
            act.wait_ge(s_pv, PAIRS - 1)
            probs_high(PAIRS - 1)
            y_high(PAIRS - 1)
            for t in range(TT):
                for c in range(2):
                    act.wait_ge(s_group, 2 * t + c + 1)
                    nc.scalar.activation(junk, out_groups[2 * t + c][2][:, :], ACT.Square,
                                         accum_out=out_sq[:, t, c:c + 1]).then_inc(s_osq, 1)
                    act.wait_ge(s_osq, 2 * t + c + 1)
                act.wait_ge(s_oms, t + 1)
                nc.scalar.activation(root[:, t:t + 1], ms[:, t:t + 1], ACT.Sqrt).then_inc(s_oroot, 1)

        @block.vector
        def _(dve):
            done = [0]

            def link(ins):
                done[0] += 1
                ins.then_inc(s_dve, 1)
                dve.wait_ge(s_dve, done[0])

            def unit_low(s, count):
                dve.wait_ge(s_hi, count)
                nc.vector.tensor_tensor(w[1][:, s, :], raw[:, s, :], w[0][:, s, :].bitcast(F32),
                                        ALU.subtract).then_inc(s_lo, 1)

            dve.wait_ge(s_small_in, 48)
            nc.vector.tensor_tensor(wfg[:, :, :], wf[:, :, :],
                                    gpre_col[:, :].unsqueeze(2).to_broadcast((P, KT, HEADS)), ALU.mult).then_inc(s_wfg, 1)
            for j in range(KT):
                if j % (KT // X_LOADS) == 0:
                    dve.wait_ge(s_x_in[j // (KT // X_LOADS)], 16)
                nc.vector.tensor_scalar(xg[0][:, j, :], x_t[:, j, :], gpre_col[:, j:j + 1], None,
                                        ALU.mult).then_inc(s_xghi, 1)
                dve.wait_ge(s_xghi, j + 1)
                nc.vector.scalar_tensor_tensor(out=xg[1][:, j, :], in0=x_t[:, j, :], scalar=gpre_col[:, j:j + 1],
                                               in1=xg[0][:, j, :].bitcast(F32), op0=ALU.mult,
                                               op1=ALU.subtract).then_inc(s_xglo, 1)
                if j == 3:
                    unit_low(0, 1)
            for s in range(1, RING):
                unit_low(s, s + 1)

            def inverse_root(n, cols, s_back, back):
                dve.wait_ge(s_back, back)
                y0, a, r, m = rstd[:, cols], newton[:, 0, cols], newton[:, 1, cols], ms[:, cols]
                link(nc.vector.reciprocal(r, root[:, cols]))
                link(nc.vector.tensor_tensor(a, r, r, ALU.mult))
                link(nc.vector.tensor_tensor(a, a, m, ALU.mult))
                link(nc.vector.tensor_scalar(a, a, -0.5, 1.5, ALU.mult, ALU.add))
                nc.vector.tensor_tensor(y0, r, a, ALU.mult).then_inc(s_rstd, 1)
                dve.wait_ge(s_rstd, n)

            dve.wait_ge(s_ssq, 1)
            nc.vector.tensor_scalar(ms[:, :], ssq_ps[:, 0:TT], 1.0 / D_MODEL, EPS, ALU.mult, ALU.add).then_inc(s_ms, 1)
            unit_low(0, 5)
            inverse_root(1, slice(0, TT), s_root, 1)
            dve.wait_ge(s_const, N_CONST)
            for t in range(TT):
                nc.vector.tensor_scalar(diag[:, t, :], ident[:, :], rstd[:, t:t + 1], None, ALU.mult).then_inc(s_diag, 1)
            unit_low(1, 6)
            dve.wait_ge(s_rbc, 1)
            nc.vector.tensor_copy(rrow[:, :], rrow_ps[:, 0:SEQ]).then_inc(s_rrow, 1)
            dve.wait_ge(s_rrow, 1)
            for j in range(KT):
                nc.vector.scalar_tensor_tensor(out=h32[:, j, :], in0=x_t[:, j, :], scalar=gpre_col[:, j:j + 1],
                                               in1=rrow[:, :], op0=ALU.mult, op1=ALU.mult).then_inc(s_h32, 1)
            def value_low(c):
                for t in range(TT):
                    dve.wait_ge(s_vhi, 2 * c + t + 1)
                    cols = slice(c * HALF, (c + 1) * HALF)
                    nc.vector.scalar_tensor_tensor(out=v[:, TT + t, cols], in0=v_banks[c][t][:, :],
                                                   scalar=rstd[:, t:t + 1], in1=v[:, t, cols].bitcast(F32),
                                                   op0=ALU.mult, op1=ALU.subtract).then_inc(s_vlo, 1)

            unit_low(2, 7)
            for c in range(2):
                dve.wait_ge(s_hhi, c + 1)
                part = slice(c * KT // 2, (c + 1) * KT // 2)
                nc.vector.tensor_tensor(h[1][:, part, :], h32[:, part, :], h[0][:, part, :].bitcast(F32),
                                        ALU.subtract).then_inc(s_hlo, 1)
            unit_low(3, 8)
            dve.wait_ge(s_f, 1)
            link(nc.vector.tensor_tensor(fz[:, 0, :], f_ps[0:HEADS, 0:SEQ], rrow[0:HEADS, :], ALU.mult))
            link(nc.vector.tensor_scalar(fz[:, 0, :], fz[:, 0, :], fb_col[:, :], None, ALU.add))
            link(nc.vector.tensor_scalar(fz[:, 1, :], fz[:, 0, :], -1.0, None, ALU.mult))
            nc.vector.tensor_tensor(fz[:, 1, :], fz[:, 1, :], fz[:, 0, :], ALU.max).then_inc(s_fabs, 1)
            link(nc.vector.tensor_scalar(f_neg, fz[:, 0, :], 0.0, 1.0 / SCALE, ALU.min, ALU.mult))
            unit_low(0, 9)
            unit_low(1, 10)
            value_low(0)
            dve.wait_ge(s_fln, 1)
            link(nc.vector.scalar_tensor_tensor(out=fz[:, 1, :], in0=fz[:, 2, :], scalar=1.0 / SCALE, in1=f_neg,
                                                op0=ALU.mult, op1=ALU.subtract))
            nc.vector.tensor_tensor_scan(fz[:, 0, :], ones_row, fz[:, 1, :], 0.0, ALU.mult, ALU.add).then_inc(s_decay, 1)
            value_low(1)

            with dve.Fori(V_UNITS // RING, QK_0 // RING) as r:
                for s in range(RING):
                    unit_low((s + 2) % RING, r * RING + s + 3)

            def probs_low(i):
                for n, (dst, src) in enumerate(((p_t0, pt0_ps), (p_t1, pt1_ps))):
                    dve.wait_ge(s_pthi, 2 * i + n + 1)
                    nc.vector.tensor_tensor(dst[1][:, :, :], src, dst[0][:, :, :].bitcast(F32),
                                            ALU.subtract).then_inc(s_ptlo, 1)

            def scores_there(i):
                dve.wait_ge(s_qk, i + 1)
                dve.wait_ge(s_bias, 2 * i + 2)

            def row_logits(i):
                for a in range(2):
                    for t, (lo, hi, ps) in enumerate(((0, P, s0_ps), (P, NB, s1_ps))):
                        c = 2 * a + t
                        nc.vector.tensor_tensor_reduce(out=logits[:, a, lo:hi], in0=ps[:, a, :], in1=bias[:, a, lo:hi],
                                                       scale=1.0, scalar=-3.0e38, op0=ALU.add, op1=ALU.max,
                                                       accum_out=mx[:, c:c + 1]).then_inc(s_logits, 1)
                    dve.wait_ge(s_logits, 4 * i + 2 * a + 2)
                    nc.vector.tensor_scalar(neg_max[:, 2 * a:2 * a + 2], mx[:, 2 * a:2 * a + 2], -SCALE, None,
                                            ALU.mult).then_inc(s_nmax, 1)

            def row_inverses(i):
                dve.wait_ge(s_exp, 4 * i + 4)
                nc.vector.reciprocal(row_inv[:, :], row_sum[:, :]).then_inc(s_inv, 1)

            def query_low(i):
                dve.wait_ge(s_qhi, i + 1)
                nc.vector.tensor_tensor(q[1][:, :], bank[0][:, 0:SEQ], q[0][:, :].bitcast(F32),
                                        ALU.subtract).then_inc(s_qlo, 1)

            def key_low(i):
                dve.wait_ge(s_khi, 2 * i + 2)
                for a in range(2):
                    rows = slice(a * HEAD_DIM, (a + 1) * HEAD_DIM)
                    nc.vector.tensor_tensor(k[1][rows, a, :], bank[1][rows, 0:SEQ], k[0][rows, a, :].bitcast(F32),
                                            ALU.subtract).then_inc(s_klo, 1)

            def gated(i):
                dve.wait_ge(s_pv, i + 1)
                for a in range(2):
                    rows = slice(a * HEAD_DIM, (a + 1) * HEAD_DIM)
                    nc.vector.tensor_tensor(y32[rows, :].unsqueeze(1), pv_ps[rows, a:a + 1, :],
                                            gate[rows, bass.ds(i, 1), :], ALU.mult).then_inc(s_y, 1)

            def attend(i, b, first=0):
                if first == 0:
                    probs_low(i - 2)
                if first != 1:
                    scores_there(i - 1)
                query_low(i)
                if first != 1:
                    row_logits(i - 1)
                unit_low((2 * b + 2) % RING, QK_0 + 3 + 2 * i)
                key_low(i)
                if first != 1:
                    row_inverses(i - 1)
                if first == 0:
                    gated(i - 2)
                unit_low((2 * b + 3) % RING, QK_0 + 4 + 2 * i)

            attend(0, 0, first=1)
            attend(1, 1, first=2)
            probs_low(0)
            scores_there(1)
            query_low(2)
            row_logits(1)
            unit_low(2, QK_0 + 7)
            key_low(2)
            row_inverses(1)
            gated(0)
            unit_low(3, QK_0 + 8)

            def attend_free(i, b):
                probs_low(i - 2)
                dve.wait_ge(s_norm, 2 * i - 2)
                scores_there(i - 1)
                query_low(i)
                row_logits(i - 1)
                unit_low((2 * b + 2) % RING, QK_0 + 3 + 2 * i)
                key_low(i)
                row_inverses(i - 1)
                dve.wait_ge(s_ylo, i - 2)
                gated(i - 2)
                unit_low((2 * b + 3) % RING, QK_0 + 4 + 2 * i)

            attend_free(3, 1)
            with dve.Fori(2, PAIRS // 2) as it:
                for b in range(2):
                    attend_free(2 * it + b, b)
            probs_low(PAIRS - 2)
            scores_there(PAIRS - 1)
            row_logits(PAIRS - 1)
            unit_low(2, UNITS + 3)
            row_inverses(PAIRS - 1)
            dve.wait_ge(s_ylo, PAIRS - 2)
            gated(PAIRS - 2)
            unit_low(3, UNITS + 4)
            probs_low(PAIRS - 1)
            dve.wait_ge(s_ylo, PAIRS - 1)
            gated(PAIRS - 1)

            dve.wait_ge(s_gpost_in, 16)
            dve.wait_ge(s_xnat_in, 16)
            for t in range(TT):
                dve.wait_ge(s_osq, 2 * t + 2)
                link(nc.vector.tensor_tensor(ms[:, t:t + 1], out_sq[:, t, 0:1], out_sq[:, t, 1:2], ALU.add))
                nc.vector.tensor_scalar(ms[:, t:t + 1], ms[:, t:t + 1], 1.0 / D_MODEL, EPS, ALU.mult,
                                        ALU.add).then_inc(s_oms, 1)
                inverse_root(t + 2, slice(t, t + 1), s_oroot, t + 1)
                for c in range(2):
                    cols = slice(c * HALF, (c + 1) * HALF)
                    fin = (probs, logits)[c][:, :, :].rearrange("p a n -> p (a n)")[:, 0:HALF]
                    if t:
                        dve.wait_ge(s_fin, c + 1)
                    link(nc.vector.scalar_tensor_tensor(out=fin, in0=out_groups[2 * t + c][2][:, :],
                                                        scalar=rstd[:, t:t + 1], in1=gpost_row[:, cols],
                                                        op0=ALU.mult, op1=ALU.mult))
                    nc.vector.tensor_tensor(x_nat[:, t, cols], x_nat[:, t, cols], fin, ALU.add).then_inc(s_fin, 1)

        @block.tensor
        def _(pe):
            def products(dst, stationary, moving, count, step=None):
                n = 0
                for j in range(count):
                    for a, b in PASSES:
                        n += 1
                        last = nc.tensor.matmul(dst, stationary(a, j), moving(b, j), start=n == 1,
                                                stop=n == count * len(PASSES))
                return last

            def value_unit(u):
                c, m = divmod(u, V_UNITS // 2)
                pe.wait_ge(s_lo, u + 1)
                if u < V_UNITS // 2:
                    pe.wait_ge(s_xglo, 2 * m + 2)
                for n in range(2):
                    j = 2 * m + n
                    for a, b in PASSES:
                        for t in range(TT):
                            last = nc.tensor.matmul(v_banks[c][t][:, :], xg[a][:, j, t * P:(t + 1) * P],
                                                    w[b][:, u % RING, n * HALF:(n + 1) * HALF],
                                                    start=j == 0 and (a, b) == PASSES[0],
                                                    stop=j == KT - 1 and (a, b) == PASSES[-1])
                last.then_inc(s_used, 1)

            pe.wait_ge(s_wfg, 1)
            for j in range(KT):
                if j % (KT // X_LOADS) == 0:
                    pe.wait_ge(s_x_in[j // (KT // X_LOADS)], 16)
                last = nc.tensor.matmul(f_ps[0:HEADS, 0:SEQ], wfg[:, j, :], x_t[:, j, :], start=j == 0, stop=j == KT - 1)
            last.then_inc(s_f, 1)

            for u in range(3):
                value_unit(u)
            pe.wait_ge(s_const, N_CONST)
            pe.wait_ge(s_sqsum, 1)
            for t in range(TT):
                last = nc.tensor.matmul(ssq_ps[:, t:t + 1], squares[:, 0, t * P:(t + 1) * P], ones[:, 0:1],
                                        start=True, stop=True)
            last.then_inc(s_ssq, 1)
            for u in range(3, 5):
                value_unit(u)
            pe.wait_ge(s_diag, TT)
            for t in range(TT):
                last = nc.tensor.matmul(rrow_ps[:, t * P:(t + 1) * P], ones[:, :], diag[:, t, :], start=True, stop=True)
            last.then_inc(s_rbc, 1)
            for u in range(5, V_UNITS):
                value_unit(u)

            def column_unit(dst, s):
                last = products(dst[:, 0:SEQ], lambda a, j: w[a][:, s, j * P:(j + 1) * P], lambda b, j: h[b][:, j, :], KT)
                last.then_inc(s_used, 1)

            pe.wait_ge(s_hlo, 2)
            pe.wait_ge(s_rrow, 1)
            for s in range(RING):
                pe.wait_ge(s_lo, V_UNITS + s + 1)
                if s >= 2:
                    pe.wait_ge(s_gate, s - 1)
                column_unit(bank[s % 2], s)
            with pe.Fori(V_UNITS // RING + 1, QK_0 // RING) as r:
                for s in range(RING):
                    pe.wait_ge(s_lo, r * RING + s + 1)
                    pe.wait_ge(s_gate, r * RING + s - V_UNITS - 1)
                    column_unit(bank[s % 2], s)

            def scores(i):
                pe.wait_ge(s_qlo, i + 1)
                pe.wait_ge(s_klo, 2 * i + 2)
                for n, (a, b) in enumerate(PASSES):
                    nc.tensor.matmul(s0_ps, q[a][:, 0:P], k[b][:, :, 0:P], start=n == 0, stop=n == 2)
                for n, (a, b) in enumerate(PASSES):
                    last = nc.tensor.matmul(s1_ps, q[a][:, P:SEQ], k[b][:, :, :], start=n == 0, stop=n == 2)
                last.then_inc(s_qk, 1)

            def transposes(i):
                pe.wait_ge(s_norm, 2 * i + 2)
                for a in range(2):
                    nc.tensor.transpose(pt0_ps[:, a, 0:P], probs[:, a, 0:P], ident[:, :])
                    nc.tensor.transpose(pt0_ps[:, a, P:SEQ], probs[:, a, P:2 * P], ident[:, :])
                    last = nc.tensor.transpose(pt1_ps[:, a, :], probs[:, a, 2 * P:3 * P], ident[:, :])
                last.then_inc(s_pt, 1)

            def values(i, b, loads):
                pe.wait_ge(s_vpair_in[b], 16 * loads)
                pe.wait_ge(s_ptlo, 2 * i + 2)
                order = [(0, PASSES[0])] + [(1, x) for x in PASSES] + [(0, x) for x in PASSES[1:]]
                for n, (t, (x, z)) in enumerate(order):
                    dst = pv_ps if t == 0 else pv_ps[:, :, P:SEQ]
                    last = nc.tensor.matmul(dst, v_pair[:, b, x * TT + t, :], (p_t0, p_t1)[t][z][:, :, :],
                                            start=n == 0, stop=n == len(order) - 1)
                last.then_inc(s_pv, 1)

            def query(i, b):
                pe.wait_ge(s_lo, QK_0 + 1 + 2 * i)
                column_unit(bank[0], 2 * b)

            def key(i, b):
                pe.wait_ge(s_lo, QK_0 + 2 + 2 * i)
                column_unit(bank[1], 2 * b + 1)

            pe.wait_ge(s_gate, G_UNITS - 1)
            query(0, 0)
            pe.wait_ge(s_gate, G_UNITS)
            key(0, 0)
            pe.wait_ge(s_qlo, 1)
            query(1, 1)
            scores(0)
            key(1, 1)

            def attend(i, b, loads, first=False):
                pe.wait_ge(s_qlo, i)
                query(i, b)
                pe.wait_ge(s_logits, 4 * i - 4)
                scores(i - 1)
                if not first:
                    pe.wait_ge(s_ptlo, 2 * i - 4)
                transposes(i - 2)
                key(i, b)
                if not first:
                    pe.wait_ge(s_y, 2 * i - 4)
                values(i - 2, b, loads)

            attend(2, 0, 1, first=True)
            attend(3, 1, 1)
            with pe.Fori(2, PAIRS // 2) as it:
                for b in range(2):
                    attend(2 * it + b, b, it)

            def out_part(g, pairs):
                t, c, dst = out_groups[g]
                cols = slice(c * HALF, (c + 1) * HALF)
                for p in pairs:
                    for a, b in PASSES:
                        wide = wo[b][:, p, cols] if p < OUT_OWN else w[b][:, p - OUT_OWN, cols]
                        last = nc.tensor.matmul(dst[:, :], y[a][:, p, t * P:(t + 1) * P], wide,
                                                start=p == 0 and (a, b) == PASSES[0],
                                                stop=p == PAIRS - 1 and (a, b) == PASSES[-1])
                return last

            pe.wait_ge(s_logits, 4 * PAIRS - 4)
            scores(PAIRS - 1)
            pe.wait_ge(s_ptlo, 2 * PAIRS - 4)
            transposes(PAIRS - 2)
            pe.wait_ge(s_olo, OUT_OWN)
            pe.wait_ge(s_lo, UNITS + 2)
            pe.wait_ge(s_ylo, PAIRS - 2)
            out_part(0, range(0, 6))
            pe.wait_ge(s_y, 2 * PAIRS - 4)
            values(PAIRS - 2, 0, PAIRS // 2)
            out_part(1, range(0, 6))
            pe.wait_ge(s_ptlo, 2 * PAIRS - 2)
            transposes(PAIRS - 1)
            out_part(2, range(0, 6))
            pe.wait_ge(s_y, 2 * PAIRS - 2)
            values(PAIRS - 1, 1, PAIRS // 2)
            pe.wait_ge(s_logits, 4 * PAIRS)
            out_part(3, range(0, 6))
            pe.wait_ge(s_lo, UNITS + 4)
            pe.wait_ge(s_ylo, PAIRS)
            for g in range(len(out_groups)):
                out_part(g, range(6, PAIRS)).then_inc(s_group, 1)


def kernel(**inputs):
    import numpy as np
    import concourse.bacc as bacc
    from concourse.bass_utils import run_bass_kernel_spmd

    x = np.asarray(inputs["x"])[0]
    w_in = np.asarray(inputs["w_in"])[0]
    group = HEADS * HEAD_DIM
    names = ["qa", "ka", "va", "ga", "fa", "qb", "kb", "vb", "gb"]
    widths = [group] * 4 + [HEADS] + [group] * 4
    starts = np.cumsum([0] + widths)
    cols = {n: w_in[:, s:s + width] for n, s, width in zip(names, starts, widths)}

    def tiles(m):
        return m.reshape(KT, P, m.shape[1]).transpose(1, 0, 2)

    units = [tiles(m)[:, 2 * n:2 * n + 2].reshape(P, UNIT) for m in (cols["va"], cols["vb"]) for n in range(KT // 2)]

    def pair_unit(kind, p):
        m = cols[kind + ("a" if p < FOX_PAIRS else "b")]
        c = (p % FOX_PAIRS) * P
        return tiles(m[:, c:c + P]).reshape(P, UNIT)

    units += [pair_unit("g", p) for p in range(PAIRS)]
    for p in range(PAIRS):
        units += [pair_unit("q", p), pair_unit("k", p)]
    arrays = {
        "xt": tiles(x.T),
        "x": x.reshape(TT, P, D_MODEL).transpose(1, 0, 2),
        "g_pre": np.asarray(inputs["norm_pre_g"])[0].reshape(KT, P).T,
        "w_units": np.stack(units),
        "w_f": tiles(cols["fa"]),
        "f_bias": np.asarray(inputs["fox_forget_b"])[0].reshape(HEADS, 1),
        "w_out": np.asarray(inputs["w_out"])[0].reshape(PAIRS, P, D_MODEL),
        "g_post": np.asarray(inputs["norm_post_g"])[0].reshape(1, D_MODEL),
    }
    arrays = {n: np.ascontiguousarray(a) for n, a in arrays.items()}
    nc = bacc.Bacc("TRN2", target_bir_lowering=False, num_devices=1)
    aps = {n: nc.dram_tensor("in_" + n, a.shape, mybir.dt.from_np(a.dtype), kind="ExternalInput").ap()
           for n, a in arrays.items()}
    aps["out"] = nc.dram_tensor("out_0", (TT, P, D_MODEL), F32, kind="ExternalOutput").ap()
    hybrid_layer(nc, **aps)
    result = run_bass_kernel_spmd(nc, [{"in_" + n: a for n, a in arrays.items()}], core_ids=[0])
    return result.results[0]["out_0"].reshape(1, SEQ, D_MODEL)
```

```python
from contextlib import ExitStack

import concourse.bass as bass
from concourse import mybir

F32 = mybir.dt.float32
F32R = mybir.dt.float32r
ALU = mybir.AluOpType
ACT = mybir.ActivationFunctionType
AX_X = mybir.AxisListType.X

P = 128
SEQ = 256
D_MODEL = 1024
HEAD_DIM = 64
HEADS = 8
KT = D_MODEL // P
TT = SEQ // P
PAIRS = 2 * HEADS // 2
FOX_PAIRS = HEADS // 2
HALF = D_MODEL // 2
UNIT = 1024
V_UNITS, G_UNITS, QK_UNITS = 8, PAIRS, 2 * PAIRS
UNITS = V_UNITS + G_UNITS + QK_UNITS
QK_0 = V_UNITS + G_UNITS
QK_0 = V_UNITS + G_UNITS
QK_0 = V_UNITS + G_UNITS
QK_0 = V_UNITS + G_UNITS
QK_0 = V_UNITS + G_UNITS
QK_0 = V_UNITS + G_UNITS
QK_0 = V_UNITS + G_UNITS
RING = 4
OUT_OWN = 4
EPS = 1e-6
SCALE = HEAD_DIM ** -0.5
MASKED = -1e32
PARTS = ("hi", "lo")
X_LOADS = 4
N_CONST = 5
PARTS = ("hi", "lo")
X_LOADS = 4
N_CONST = 5
PARTS = ("hi", "lo")
X_LOADS = 4
N_CONST = 5
PARTS = ("hi", "lo")
X_LOADS = 4
N_CONST = 5
PARTS = ("hi", "lo")
X_LOADS = 4
N_CONST = 5
PARTS = ("hi", "lo")
X_LOADS = 4
N_CONST = 5
PARTS = ("hi", "lo")
X_LOADS = 4
N_CONST = 5
PASSES = ((0, 0), (0, 1), (1, 0))
NB = P + SEQ


def hybrid_layer(nc, xt, x, g_pre, w_units, w_f, f_bias, w_out, g_post, out):
    ctx = ExitStack()

    def sb(name, shape, dt=F32):
        return ctx.enter_context(nc.sbuf_tensor(name, shape, dt))

    def sem(name):
        return ctx.enter_context(nc.semaphore(name))

    with ctx:
        x_t = sb("x_t", [P, KT, SEQ])
        xg = [sb(f"xg_{n}", [P, KT, SEQ], F32R) for n in PARTS]
        h32 = sb("h32", [P, KT, SEQ])
        h = [sb(f"h_{n}", [P, KT, SEQ], F32R) for n in PARTS]
        squares = sb("squares", [P, KT, SEQ])
        gpre_col = sb("gpre_col", [P, KT])
        gpost_row = sb("gpost_row", [P, D_MODEL])
        wf = sb("wf", [P, KT, HEADS])
        wfg = sb("wfg", [P, KT, HEADS])
        fb_col = sb("fb_col", [HEADS, 1])
        raw = sb("raw", [P, RING, UNIT])
        w = [sb(f"w_{n}", [P, RING, UNIT], F32R) for n in PARTS]
        raw_out = sb("raw_out", [P, UNIT])
        wo = [sb(f"wo_{n}", [P, OUT_OWN, D_MODEL], F32R) for n in PARTS]
        v = sb("v", [P, 2 * TT, D_MODEL], F32R)
        v_pair = sb("v_pair", [P, 2, 2 * TT, P], F32R)
        q = [sb(f"q_{n}", [P, SEQ], F32R) for n in PARTS]
        k = [sb(f"k_{n}", [P, 2, SEQ], F32R) for n in PARTS]
        bias = sb("bias", [P, 2, NB])
        logits = sb("logits", [P, 2, NB])
        probs = sb("probs", [P, 2, NB])
        p_t0 = [sb(f"p_t0_{n}", [P, 2, SEQ], F32R) for n in PARTS]
        p_t1 = [sb(f"p_t1_{n}", [P, 2, P], F32R) for n in PARTS]
        gate = sb("gate", [P, PAIRS, SEQ])
        y32 = sb("y32", [P, SEQ])
        ident = sb("ident", [P, P])
        ones = sb("ones", [P, P])
        causal = sb("causal", [P, NB])
        dist = sb("dist", [P, NB])
        slope_col = sb("slope_col", [P, HEADS])
        diag = sb("diag", [P, TT, P])
        rrow = sb("rrow", [P, SEQ])
        ms = sb("ms", [P, TT])
        root = sb("root", [P, TT])
        rstd = sb("rstd", [P, TT])
        newton = sb("newton", [P, 2, TT])
        mx = sb("mx", [P, 4])
        neg_max = sb("neg_max", [P, 4])
        row_sum = sb("row_sum", [P, 4])
        row_inv = sb("row_inv", [P, 4])
        out_sq = sb("out_sq", [P, TT, 2])
        y = xg
        decay = squares
        x_nat = x_t[:, :, :].rearrange("p a b -> p (a b)").rearrange("p (t d) -> p t d", t=TT)
        fz = logits[0:HEADS, :, :].rearrange("p a n -> p (a n)").rearrange("p (a n) -> p a n", n=SEQ)
        ones_row = probs[0:HEADS, 0, 0:SEQ]
        f_neg = probs[0:HEADS, 1, 0:SEQ]
        scaled = [m[:, :, :].rearrange("p a n -> p (a n)")[:, 0:HALF] for m in (probs, logits)]
        junk = bias[:, :, :].rearrange("p a n -> p (a n)")[:, 0:HALF]
        decay_dram = nc.dram_tensor("decay_rows_scratch", (HEADS, SEQ), F32, kind="Internal").ap()

        bank = [ctx.enter_context(nc.psum_tensor(f"bank{b}", [P, HALF], F32)) for b in range(8)]
        v_banks = [[bank[2], bank[3]], [bank[4], bank[5]]]
        ssq_ps, rrow_ps, f_ps = bank[6], bank[1], bank[7]
        s0_ps = bank[2][:, 0:2 * P].rearrange("p (a n) -> p a n", a=2)
        s1_ps = bank[3][:, :].rearrange("p (a n) -> p a n", a=2)
        pt0_ps = bank[4][:, :].rearrange("p (a n) -> p a n", a=2)
        pt1_ps = bank[5][:, 0:2 * P].rearrange("p (a n) -> p a n", a=2)
        pv_ps = bank[6][:, :].rearrange("p (a n) -> p a n", a=2)
        out_groups = [(0, 0, bank[7]), (0, 1, bank[0]), (1, 0, bank[1]), (1, 1, bank[2])]

        def group_bank(t, c):
            return out_groups[2 * t + c][2]

        s_small_in = sem("small_in")
        s_x_in = [sem(f"x_in{c}") for c in range(X_LOADS)]
        s_gpost_in, s_xnat_in = sem("gpost_in"), sem("x_nat_in")
        s_raw_in = [sem(f"raw_in{s}") for s in range(RING)]
        s_raw_out_in = sem("raw_out_in")
        s_vpair_in = [sem(f"v_pair_in{s}") for s in range(2)]
        s_hi, s_lo = sem("unit_hi"), sem("unit_lo")
        s_used = sem("unit_used")
        s_ohi, s_olo = sem("out_unit_hi"), sem("out_unit_lo")
        s_pool, s_dve = sem("pool_chain"), sem("dve_chain")
        s_const = sem("constants")
        s_xghi, s_xglo = sem("xg_hi"), sem("xg_lo")
        s_wfg, s_f = sem("wfg_ready"), sem("f_ready")
        s_sq, s_sqsum, s_ssq = sem("squares_done"), sem("square_sums"), sem("ssq_ready")
        s_ms, s_root, s_rstd = sem("mean_square"), sem("root_ready"), sem("rstd_ready")
        s_diag, s_rbc, s_rrow = sem("diag_ready"), sem("rstd_broadcast"), sem("rrow_ready")
        s_fabs, s_fexp, s_fln = sem("f_abs"), sem("f_exp"), sem("f_ln")
        s_decay, s_decay_st, s_decay_in = sem("decay_rows"), sem("decay_stored"), sem("decay_in")
        s_h32, s_hhi, s_hlo = sem("h32_ready"), sem("h_hi"), sem("h_lo")
        s_vhi, s_vlo = sem("v_hi"), sem("v_lo")
        s_gmul, s_gate = sem("gate_products"), sem("gates_ready")
        s_qhi, s_qlo = sem("q_hi"), sem("q_lo")
        s_khi, s_klo = sem("k_hi"), sem("k_lo")
        s_qk = sem("scores_ready")
        s_bias = sem("bias_ready")
        s_logits = sem("logits_ready")
        s_nmax = sem("neg_max_ready")
        s_exp = sem("exp_done")
        s_inv, s_norm = sem("row_inv_ready"), sem("probs_normed")
        s_pt = sem("probs_transposed")
        s_pthi, s_ptlo = sem("pt_hi"), sem("pt_lo")
        s_pv = sem("pv_ready")
        s_y, s_yhi, s_ylo = sem("y_ready"), sem("y_hi"), sem("y_lo")
        s_group = sem("out_group")
        s_osq, s_oms, s_oroot = sem("out_squares"), sem("out_mean_square"), sem("out_root")
        s_scaled = [sem(f"scaled{c}") for c in range(2)]
        s_fin = [sem(f"fin_ready{c}") for c in range(2)]
        s_stored = sem("stored")

        block = ctx.enter_context(nc.Block())

        @block.sync
        def _(sp):
            sp.dma_start(gpre_col[:, :], g_pre).then_inc(s_small_in, 16)
            sp.dma_start(wf[:, :, :], w_f).then_inc(s_small_in, 16)
            sp.dma_start(fb_col[:, :], f_bias).then_inc(s_small_in, 16)
            n = KT // X_LOADS
            for c in range(X_LOADS):
                sp.dma_start(x_t[:, n * c:n * c + n, :], xt[:, n * c:n * c + n, :]).then_inc(s_x_in[c], 16)
            for s in range(RING):
                sp.dma_start(raw[:, s, :], w_units[s]).then_inc(s_raw_in[s], 16)

            def load_unit(r, s):
                sp.wait_ge(s_lo, r * RING + s + 1 - RING)
                sp.dma_start(raw[:, s, :], w_units[r * RING + s]).then_inc(s_raw_in[s], 16)

            for s in range(RING):
                load_unit(1, s)
            for u in range(V_UNITS, QK_0 + RING):
                load_unit(u // RING, u % RING)
                j = (u - V_UNITS - 3) // 2
                if u % 2 and 0 <= j < OUT_OWN:
                    if j:
                        sp.wait_ge(s_olo, j)
                    sp.dma_start(raw_out[:, :], w_out[j]).then_inc(s_raw_out_in, 16)
            sp.dma_start(gpost_row[:, :], g_post[0:1, :].to_broadcast((P, D_MODEL))).then_inc(s_gpost_in, 16)
            with sp.Fori(QK_0 // RING + 1, UNITS // RING) as r:
                for s in range(RING):
                    load_unit(r, s)
            for s in range(RING):
                sp.wait_ge(s_lo, UNITS + s + 1 - RING)
                sp.dma_start(raw[:, s, :], w_out[OUT_OWN + s]).then_inc(s_raw_in[s], 16)
            sp.wait_ge(s_h32, KT)
            sp.dma_start(x_nat, x).then_inc(s_xnat_in, 16)
            for t in range(TT):
                for c in range(2):
                    sp.wait_ge(s_fin[c], t + 1)
                    sp.dma_start(out[t, :, c * HALF:(c + 1) * HALF],
                                 x_nat[:, t, c * HALF:(c + 1) * HALF]).then_inc(s_stored, 16)
            sp.wait_ge(s_stored, 16 * len(out_groups))

        @block.gpsimd
        def _(pool):
            done = [0]

            def link(ins):
                done[0] += 1
                ins.then_inc(s_pool, 1)
                pool.wait_ge(s_pool, done[0])

            link(pool.memset(ident[:, :], 0.0))
            pool.affine_select(out=ident[:, :], in_=ident[:, :], compare_op=ALU.not_equal, fill=1.0,
                               base=0, pattern=[[-1, P]], channel_multiplier=1).then_inc(s_const, 1)
            pool.memset(ones[:, :], 1.0).then_inc(s_const, 1)
            for n in range(2):
                pool.memset(k[n][:, :, :].bitcast(F32), 0.0).then_inc(s_const, 1)
            pool.memset(ones_row, 1.0).then_inc(s_const, 1)
            pool.memset(causal[:, :], 0.0).then_inc(s_pool, 1)
            pool.iota(dist[:, 0:P], pattern=[[1, P]], base=0, channel_multiplier=-1,
                      allow_small_or_imprecise_dtypes=True).then_inc(s_pool, 1)
            pool.iota(dist[:, P:NB], pattern=[[1, SEQ]], base=-P, channel_multiplier=-1,
                      allow_small_or_imprecise_dtypes=True).then_inc(s_pool, 1)
            for n in range(HEADS):
                pool.memset(slope_col[:, n:n + 1], 2.0 ** (-8.0 * (n + 1) / HEADS) / SCALE).then_inc(s_pool, 1)
            done[0] += 3 + HEADS
            pool.wait_ge(s_pool, done[0])
            for m in (causal, dist):
                for lo, hi, base in ((0, P, 0), (P, NB, P)):
                    pool.affine_select(out=m[:, lo:hi], in_=m[:, lo:hi], compare_op=ALU.is_ge, fill=MASKED,
                                       base=base, pattern=[[-1, hi - lo]], channel_multiplier=1).then_inc(s_pool, 1)
                    done[0] += 1

            pool.wait_ge(s_sq, X_LOADS)
            n = KT // 2
            while n > 1:
                link(pool.tensor_tensor(squares[:, 0:n, :], squares[:, 0:n, :], squares[:, n:2 * n, :], ALU.add))
                n //= 2
            pool.tensor_tensor(squares[:, 0, :], squares[:, 0, :], squares[:, 1, :], ALU.add).then_inc(s_sqsum, 1)

            with pool.Fori(0, OUT_OWN) as j:
                pool.wait_ge(s_ohi, j + 1)
                pool.tensor_tensor(wo[1][:, bass.ds(j, 1), :], raw_out[:, :].unsqueeze(1),
                                   wo[0][:, bass.ds(j, 1), :].bitcast(F32), ALU.subtract).then_inc(s_olo, 1)

            def fox_bias(i):
                for lo, hi in ((0, P), (P, NB)):
                    last = pool.tensor_tensor(bias[:, :, lo:hi], decay[:, bass.ds(2 * i, 2), 0:hi - lo],
                                              causal[:, lo:hi].unsqueeze(1).to_broadcast((P, 2, hi - lo)), ALU.add)
                    if lo == 0:
                        last.then_inc(s_bias, 1)
                last.then_inc(s_bias, 1)

            def moba_bias(i):
                for lo, hi in ((0, P), (P, NB)):
                    pool.tensor_tensor(bias[:, :, lo:hi],
                                       dist[:, lo:hi].unsqueeze(1).to_broadcast((P, 2, hi - lo)),
                                       slope_col[:, bass.ds(2 * i - HEADS, 2)].unsqueeze(2).to_broadcast((P, 2, hi - lo)),
                                       ALU.mult).then_inc(s_bias, 1)

            def norm_probs(i):
                pool.wait_ge(s_inv, i + 1)
                for t, (lo, hi) in enumerate(((0, P), (P, NB))):
                    pool.tensor_tensor(probs[:, :, lo:hi], probs[:, :, lo:hi],
                                       row_inv[:, t::2].unsqueeze(2).to_broadcast((P, 2, hi - lo)),
                                       ALU.mult).then_inc(s_norm, 1)

            def y_low(i):
                pool.wait_ge(s_yhi, i + 1)
                pool.tensor_tensor(y[1][:, bass.ds(i, 1), :], y32[:, :].unsqueeze(1),
                                   y[0][:, bass.ds(i, 1), :].bitcast(F32), ALU.subtract).then_inc(s_ylo, 1)

            pool.wait_ge(s_pool, done[0])
            pool.wait_ge(s_decay_in, 16)
            fox_bias(0)
            pool.wait_ge(s_logits, 4)
            fox_bias(1)
            norm_probs(0)
            with pool.Fori(2, FOX_PAIRS) as i:
                pool.wait_ge(s_logits, 4 * i)
                fox_bias(i)
                norm_probs(i - 1)
                y_low(i - 2)
            with pool.Fori(FOX_PAIRS, PAIRS) as i:
                pool.wait_ge(s_logits, 4 * i)
                moba_bias(i)
                norm_probs(i - 1)
                y_low(i - 2)
            norm_probs(PAIRS - 1)
            y_low(PAIRS - 2)
            y_low(PAIRS - 1)
            for t in range(TT):
                pool.wait_ge(s_xnat_in, 16)
                pool.wait_ge(s_scaled[1], t + 1)
                pool.tensor_tensor(x_nat[:, t, HALF:], x_nat[:, t, HALF:], scaled[1], ALU.add).then_inc(s_fin[1], 1)

        @block.scalar
        def _(act):
            def unit_high(s, n, used=None):
                act.wait_ge(s_raw_in[s], n)
                if used is not None:
                    act.wait_ge(s_used, used)
                nc.scalar.activation(w[0][:, s, :], raw[:, s, :], ACT.Copy).then_inc(s_hi, 1)

            def out_unit_high(j):
                act.wait_ge(s_raw_out_in, 16 * (j + 1))
                nc.scalar.activation(wo[0][:, bass.ds(j, 1), :], raw_out[:, :].unsqueeze(1), ACT.Copy).then_inc(s_ohi, 1)

            act.wait_ge(s_small_in, 48)
            for j in range(KT):
                act.wait_ge(s_x_in[j // (KT // X_LOADS)], 16)
                nc.scalar.activation(xg[0][:, j, :], x_t[:, j, :], ACT.Copy, scale=gpre_col[:, j:j + 1]).then_inc(s_xghi, 1)
            unit_high(0, 16)
            unit_high(1, 16)
            n = KT // X_LOADS
            for c in range(X_LOADS):
                nc.scalar.activation(squares[:, n * c:n * c + n, :], x_t[:, n * c:n * c + n, :],
                                     ACT.Square).then_inc(s_sq, 1)
            unit_high(2, 16)
            unit_high(3, 16)
            unit_high(0, 32, 1)
            unit_high(1, 32, 2)
            act.wait_ge(s_ms, 1)
            nc.scalar.activation(root[:, :], ms[:, :], ACT.Sqrt).then_inc(s_root, 1)
            unit_high(2, 32, 3)

            def value_high(c):
                act.wait_ge(s_used, 4 * c + 4)
                act.wait_ge(s_rstd, 1)
                for t in range(TT):
                    nc.scalar.activation(v[:, t, c * HALF:(c + 1) * HALF], v_banks[c][t][:, :], ACT.Copy,
                                         scale=rstd[:, t:t + 1]).then_inc(s_vhi, 1)

            unit_high(3, 32, 4)
            value_high(0)
            unit_high(0, 48, 5)
            act.wait_ge(s_fabs, 1)
            nc.scalar.activation(fz[:, 1, :], fz[:, 1, :], ACT.Exp, scale=-1.0).then_inc(s_fexp, 1)
            act.wait_ge(s_fexp, 1)
            nc.scalar.activation(fz[:, 2, :], fz[:, 1, :], ACT.Ln, bias=1.0).then_inc(s_fln, 1)
            unit_high(1, 48, 6)
            act.wait_ge(s_decay, 1)
            act.dma_start(decay_dram, fz[:, 0, :]).then_inc(s_decay_st, 16)

            def gate_round(r):
                for s in range(RING):
                    unit_high((s + 2) % RING, 16 * (r + 1 + (s + 2) // RING), r * RING + s - 1)
                    if r == V_UNITS // RING and s == 0:
                        value_high(1)
                    if s % 2:
                        out_unit_high(r * 2 - V_UNITS // 2 + s // 2)

            gate_round(V_UNITS // RING)
            act.wait_ge(s_decay_st, 16)
            act.dma_start(decay[:, :, :], decay_dram.partition_broadcast(P)).then_inc(s_decay_in, 16)
            for c in range(2):
                act.wait_ge(s_h32, (c + 1) * KT // 2)
                nc.scalar.activation(h[0][:, c * KT // 2:(c + 1) * KT // 2, :],
                                     h32[:, c * KT // 2:(c + 1) * KT // 2, :], ACT.Copy).then_inc(s_hhi, 1)
            gate_round(V_UNITS // RING + 1)

            def fetch_values(i, b):
                act.dma_start(v_pair[:, b, :, :].bitcast(F32), v[:, :, bass.ds(i * P, P)].bitcast(F32)).then_inc(s_vpair_in[b], 16)

            def probs_high(i):
                act.wait_ge(s_pt, i + 1)
                nc.scalar.activation(p_t0[0][:, :, :], pt0_ps, ACT.Copy).then_inc(s_pthi, 1)
                nc.scalar.activation(p_t1[0][:, :, :], pt1_ps, ACT.Copy).then_inc(s_pthi, 1)

            def exps(i):
                for a in range(2):
                    act.wait_ge(s_nmax, 2 * i + a + 1)
                    for t, (lo, hi) in enumerate(((0, P), (P, NB))):
                        c = 2 * a + t
                        nc.scalar.activation(probs[:, a, lo:hi], logits[:, a, lo:hi], ACT.Exp,
                                             bias=neg_max[:, c:c + 1], scale=SCALE,
                                             accum_out=row_sum[:, c:c + 1]).then_inc(s_exp, 1)

            def y_high(i):
                act.wait_ge(s_y, 2 * i + 2)
                nc.scalar.activation(y[0][:, bass.ds(i, 1), :], y32[:, :].unsqueeze(1), ACT.Copy).then_inc(s_yhi, 1)

            def query_high(i):
                act.wait_ge(s_used, QK_0 + 1 + 2 * i)
                nc.scalar.activation(q[0][:, :], bank[0][:, 0:SEQ], ACT.Copy).then_inc(s_qhi, 1)

            def key_high(i):
                act.wait_ge(s_used, QK_0 + 2 + 2 * i)
                for a in range(2):
                    rows = slice(a * HEAD_DIM, (a + 1) * HEAD_DIM)
                    nc.scalar.activation(k[0][rows, a, :], bank[1][rows, 0:SEQ], ACT.Copy).then_inc(s_khi, 1)

            def gates_silu():
                act.wait_ge(s_gmul, PAIRS)
                nc.scalar.activation(gate[:, :, :], gate[:, :, :], ACT.Silu).then_inc(s_gate, 1)

            def attend(i, b, n, first=0, fresh=False):
                unit_high((2 * b + 2) % RING, n, 2 * i + QK_0 - 1)
                if first == 0 and not fresh:
                    act.wait_ge(s_pv, i - 2)
                if first != 1:
                    fetch_values(i - 1, 1 - b)
                    act.wait_ge(s_qk, i)
                query_high(i)
                if first == 0:
                    probs_high(i - 2)
                if first != 1:
                    exps(i - 1)
                if first == 1:
                    gates_silu()
                key_high(i)
                unit_high((2 * b + 3) % RING, n, 2 * i + QK_0)
                if first == 0:
                    y_high(i - 2)

            act.wait_ge(s_const, N_CONST)
            attend(0, 0, 16 * (QK_0 // RING + 1), first=1)
            act.wait_ge(s_vlo, 4)
            attend(1, 1, 16 * (QK_0 // RING + 2), first=2)
            attend(2, 0, 16 * (QK_0 // RING + 2), fresh=True)
            attend(3, 1, 16 * (QK_0 // RING + 3))
            with act.Fori(2, PAIRS // 2) as it:
                for b in range(2):
                    attend(2 * it + b, b, 16 * (it + QK_0 // RING + 1 + b))
            unit_high(2, 16 * (UNITS // RING + 1), UNITS - 1)
            act.wait_ge(s_pv, PAIRS - 2)
            fetch_values(PAIRS - 1, 1)
            probs_high(PAIRS - 2)
            exps(PAIRS - 1)
            unit_high(3, 16 * (UNITS // RING + 1), UNITS)
            y_high(PAIRS - 2)
            act.wait_ge(s_pv, PAIRS - 1)
            probs_high(PAIRS - 1)
            y_high(PAIRS - 1)
            nc.scalar.activation(junk[:, 0:1], rstd[:, 0:1], ACT.Sqrt).then_inc(s_osq, 1)
            act.wait_ge(s_osq, 1)
            for t in range(TT):
                for c in range(2):
                    act.wait_ge(s_group, 2 * t + c + 1)
                    nc.scalar.activation(junk, group_bank(t, c)[:, :], ACT.Square,
                                         accum_out=out_sq[:, t, c:c + 1]).then_inc(s_osq, 1)
                    act.wait_ge(s_osq, 2 * t + c + 2)
                act.wait_ge(s_oms, t + 1)
                nc.scalar.activation(root[:, t:t + 1], ms[:, t:t + 1], ACT.Sqrt).then_inc(s_oroot, 1)

        @block.vector
        def _(dve):
            done = [0]

            def link(ins):
                done[0] += 1
                ins.then_inc(s_dve, 1)
                dve.wait_ge(s_dve, done[0])

            def unit_low(s, count):
                dve.wait_ge(s_hi, count)
                nc.vector.tensor_tensor(w[1][:, s, :], raw[:, s, :], w[0][:, s, :].bitcast(F32),
                                        ALU.subtract).then_inc(s_lo, 1)

            dve.wait_ge(s_small_in, 48)
            nc.vector.tensor_tensor(wfg[:, :, :], wf[:, :, :],
                                    gpre_col[:, :].unsqueeze(2).to_broadcast((P, KT, HEADS)), ALU.mult).then_inc(s_wfg, 1)
            for j in range(KT):
                dve.wait_ge(s_xghi, j + 1)
                nc.vector.scalar_tensor_tensor(out=xg[1][:, j, :], in0=x_t[:, j, :], scalar=gpre_col[:, j:j + 1],
                                               in1=xg[0][:, j, :].bitcast(F32), op0=ALU.mult,
                                               op1=ALU.subtract).then_inc(s_xglo, 1)
            for u in range(6):
                unit_low(u % RING, u + 1)

            dve.wait_ge(s_ssq, 1)
            nc.vector.tensor_scalar(ms[:, :], ssq_ps[:, 0:TT], 1.0 / D_MODEL, EPS, ALU.mult, ALU.add).then_inc(s_ms, 1)
            dve.wait_ge(s_root, 1)
            inv, step = newton[:, 0, :], newton[:, 1, :]
            link(nc.vector.reciprocal(inv, root[:, :]))
            link(nc.vector.tensor_tensor(step, inv, inv, ALU.mult))
            link(nc.vector.tensor_tensor(step, step, ms[:, :], ALU.mult))
            link(nc.vector.tensor_scalar(step, step, -0.5, 1.5, ALU.mult, ALU.add))
            nc.vector.tensor_tensor(rstd[:, :], inv, step, ALU.mult).then_inc(s_rstd, 1)
            dve.wait_ge(s_rstd, 1)
            dve.wait_ge(s_const, N_CONST)
            for t in range(TT):
                nc.vector.tensor_scalar(diag[:, t, :], ident[:, :], rstd[:, t:t + 1], None, ALU.mult).then_inc(s_diag, 1)
            unit_low(2, 7)
            unit_low(3, 8)

            def value_low(c):
                for t in range(TT):
                    dve.wait_ge(s_vhi, 2 * c + t + 1)
                    cols = slice(c * HALF, (c + 1) * HALF)
                    nc.vector.scalar_tensor_tensor(out=v[:, TT + t, cols], in0=v_banks[c][t][:, :],
                                                   scalar=rstd[:, t:t + 1], in1=v[:, t, cols].bitcast(F32),
                                                   op0=ALU.mult, op1=ALU.subtract).then_inc(s_vlo, 1)

            dve.wait_ge(s_rbc, 1)
            nc.vector.tensor_copy(rrow[:, :], rrow_ps[:, 0:SEQ]).then_inc(s_rrow, 1)
            dve.wait_ge(s_rrow, 1)
            dve.wait_ge(s_f, 1)
            link(nc.vector.tensor_tensor(fz[:, 0, :], f_ps[0:HEADS, 0:SEQ], rrow[0:HEADS, :], ALU.mult))
            link(nc.vector.tensor_scalar(fz[:, 0, :], fz[:, 0, :], fb_col[:, :], None, ALU.add))
            link(nc.vector.tensor_scalar(fz[:, 1, :], fz[:, 0, :], -1.0, None, ALU.mult))
            nc.vector.tensor_tensor(fz[:, 1, :], fz[:, 1, :], fz[:, 0, :], ALU.max).then_inc(s_fabs, 1)
            link(nc.vector.tensor_scalar(f_neg, fz[:, 0, :], 0.0, 1.0 / SCALE, ALU.min, ALU.mult))
            unit_low(0, 9)
            value_low(0)
            unit_low(1, 10)
            dve.wait_ge(s_fln, 1)
            link(nc.vector.scalar_tensor_tensor(out=fz[:, 1, :], in0=fz[:, 2, :], scalar=1.0 / SCALE, in1=f_neg,
                                                op0=ALU.mult, op1=ALU.subtract))
            nc.vector.tensor_tensor_scan(fz[:, 0, :], ones_row, fz[:, 1, :], 0.0, ALU.mult, ALU.add).then_inc(s_decay, 1)

            def gate_round(r):
                for s in range(RING):
                    unit_low((s + 2) % RING, r * RING + s + 3)
                    if r == V_UNITS // RING:
                        if s == 0:
                            value_low(1)
                        for j in (2 * s, 2 * s + 1):
                            nc.vector.scalar_tensor_tensor(out=h32[:, j, :], in0=x_t[:, j, :],
                                                           scalar=gpre_col[:, j:j + 1], in1=rrow[:, :],
                                                           op0=ALU.mult, op1=ALU.mult).then_inc(s_h32, 1)
                    elif s < 2:
                        dve.wait_ge(s_hhi, s + 1)
                        part = slice(s * KT // 2, (s + 1) * KT // 2)
                        nc.vector.tensor_tensor(h[1][:, part, :], h32[:, part, :], h[0][:, part, :].bitcast(F32),
                                                ALU.subtract).then_inc(s_hlo, 1)
                    u = r * RING + s
                    dve.wait_ge(s_used, u + 1)
                    nc.vector.tensor_tensor(gate[:, u - V_UNITS, :], bank[s % 2][:, 0:SEQ], rrow[:, :],
                                            ALU.mult).then_inc(s_gmul, 1)

            gate_round(V_UNITS // RING)
            gate_round(V_UNITS // RING + 1)

            def probs_low(i):
                for n, (dst, src) in enumerate(((p_t0, pt0_ps), (p_t1, pt1_ps))):
                    dve.wait_ge(s_pthi, 2 * i + n + 1)
                    nc.vector.tensor_tensor(dst[1][:, :, :], src, dst[0][:, :, :].bitcast(F32),
                                            ALU.subtract).then_inc(s_ptlo, 1)

            def scores_there(i):
                dve.wait_ge(s_qk, i + 1)
                dve.wait_ge(s_bias, 2 * i + 2)

            def row_logits(i, a):
                for t, (lo, hi, ps) in enumerate(((0, P, s0_ps), (P, NB, s1_ps))):
                    c = 2 * a + t
                    nc.vector.tensor_tensor_reduce(out=logits[:, a, lo:hi], in0=ps[:, a, :], in1=bias[:, a, lo:hi],
                                                   scale=1.0, scalar=-3.0e38, op0=ALU.add, op1=ALU.max,
                                                   accum_out=mx[:, c:c + 1]).then_inc(s_logits, 1)
                dve.wait_ge(s_logits, 4 * i + 2 * a + 2)
                nc.vector.tensor_scalar(neg_max[:, 2 * a:2 * a + 2], mx[:, 2 * a:2 * a + 2], -SCALE, None,
                                        ALU.mult).then_inc(s_nmax, 1)

            def row_inverses(i):
                dve.wait_ge(s_exp, 4 * i + 4)
                nc.vector.reciprocal(row_inv[:, :], row_sum[:, :]).then_inc(s_inv, 1)

            def query_low(i):
                dve.wait_ge(s_qhi, i + 1)
                nc.vector.tensor_tensor(q[1][:, :], bank[0][:, 0:SEQ], q[0][:, :].bitcast(F32),
                                        ALU.subtract).then_inc(s_qlo, 1)

            def key_low(i):
                dve.wait_ge(s_khi, 2 * i + 2)
                for a in range(2):
                    rows = slice(a * HEAD_DIM, (a + 1) * HEAD_DIM)
                    nc.vector.tensor_tensor(k[1][rows, a, :], bank[1][rows, 0:SEQ], k[0][rows, a, :].bitcast(F32),
                                            ALU.subtract).then_inc(s_klo, 1)

            def gated(i):
                dve.wait_ge(s_pv, i + 1)
                for a in range(2):
                    rows = slice(a * HEAD_DIM, (a + 1) * HEAD_DIM)
                    nc.vector.tensor_tensor(y32[rows, :].unsqueeze(1), pv_ps[rows, a:a + 1, :],
                                            gate[rows, bass.ds(i, 1), :], ALU.mult).then_inc(s_y, 1)

            def attend(i, b, first=0):
                unit_low((2 * b + 2) % RING, QK_0 + 3 + 2 * i)
                if first == 0 and not (isinstance(i, int) and i == 2):
                    dve.wait_ge(s_norm, 2 * i - 2)
                if first != 1:
                    scores_there(i - 1)
                query_low(i)
                if first != 1:
                    row_logits(i - 1, 0)
                if first == 0:
                    probs_low(i - 2)
                if first != 1:
                    row_logits(i - 1, 1)
                key_low(i)
                if first != 1:
                    row_inverses(i - 1)
                if first == 0:
                    if not (isinstance(i, int) and i == 2):
                        dve.wait_ge(s_ylo, i - 2)
                    gated(i - 2)
                unit_low((2 * b + 3) % RING, QK_0 + 4 + 2 * i)

            attend(0, 0, first=1)
            attend(1, 1, first=2)
            dve.wait_ge(s_gate, 1)
            attend(2, 0)
            attend(3, 1)
            with dve.Fori(2, PAIRS // 2) as it:
                for b in range(2):
                    attend(2 * it + b, b)
            unit_low(2, UNITS + 3)
            scores_there(PAIRS - 1)
            row_logits(PAIRS - 1, 0)
            probs_low(PAIRS - 2)
            row_logits(PAIRS - 1, 1)
            row_inverses(PAIRS - 1)
            dve.wait_ge(s_ylo, PAIRS - 2)
            gated(PAIRS - 2)
            unit_low(3, UNITS + 4)
            probs_low(PAIRS - 1)
            dve.wait_ge(s_ylo, PAIRS - 1)
            gated(PAIRS - 1)

            dve.wait_ge(s_gpost_in, 16)
            dve.wait_ge(s_xnat_in, 16)
            for t in range(TT):
                r, a, m = newton[:, 0, t:t + 1], newton[:, 1, t:t + 1], ms[:, t:t + 1]
                dve.wait_ge(s_osq, 2 * t + 2)
                link(nc.vector.tensor_scalar(a, out_sq[:, t, 0:1], 1.0 / D_MODEL, EPS, ALU.mult, ALU.add))
                dve.wait_ge(s_osq, 2 * t + 3)
                nc.vector.scalar_tensor_tensor(out=m, in0=out_sq[:, t, 1:2], scalar=1.0 / D_MODEL, in1=a,
                                               op0=ALU.mult, op1=ALU.add).then_inc(s_oms, 1)
                dve.wait_ge(s_oms, t + 1)
                dve.wait_ge(s_oroot, t + 1)
                link(nc.vector.reciprocal(r, root[:, t:t + 1]))
                link(nc.vector.scalar_tensor_tensor(out=a, in0=r, scalar=m, in1=r, op0=ALU.mult, op1=ALU.mult))
                link(nc.vector.tensor_scalar(a, a, -0.5, 1.5, ALU.mult, ALU.add))
                nc.vector.tensor_tensor(rstd[:, t:t + 1], r, a, ALU.mult).then_inc(s_rstd, 1)
                dve.wait_ge(s_rstd, t + 2)
                for c in (1, 0):
                    cols = slice(c * HALF, (c + 1) * HALF)
                    if t:
                        dve.wait_ge(s_fin[c], 1)
                    nc.vector.scalar_tensor_tensor(out=scaled[c], in0=group_bank(t, c)[:, :],
                                                   scalar=rstd[:, t:t + 1], in1=gpost_row[:, cols],
                                                   op0=ALU.mult, op1=ALU.mult).then_inc(s_scaled[c], 1)
                dve.wait_ge(s_scaled[0], t + 1)
                nc.vector.tensor_tensor(x_nat[:, t, 0:HALF], x_nat[:, t, 0:HALF], scaled[0], ALU.add).then_inc(s_fin[0], 1)

        @block.tensor
        def _(pe):
            def products(dst, stationary, moving, count, step=None):
                n = 0
                for j in range(count):
                    for a, b in PASSES:
                        n += 1
                        last = nc.tensor.matmul(dst, stationary(a, j), moving(b, j), start=n == 1,
                                                stop=n == count * len(PASSES))
                return last

            def value_unit(u):
                c, m = divmod(u, V_UNITS // 2)
                pe.wait_ge(s_lo, u + 1)
                if u < V_UNITS // 2:
                    pe.wait_ge(s_xglo, 2 * m + 2)
                for n in range(2):
                    j = 2 * m + n
                    for a, b in PASSES:
                        for t in range(TT):
                            last = nc.tensor.matmul(v_banks[c][t][:, :], xg[a][:, j, t * P:(t + 1) * P],
                                                    w[b][:, u % RING, n * HALF:(n + 1) * HALF],
                                                    start=j == 0 and (a, b) == PASSES[0],
                                                    stop=j == KT - 1 and (a, b) == PASSES[-1])
                last.then_inc(s_used, 1)

            pe.wait_ge(s_wfg, 1)
            for j in range(KT):
                if j % (KT // X_LOADS) == 0:
                    pe.wait_ge(s_x_in[j // (KT // X_LOADS)], 16)
                last = nc.tensor.matmul(f_ps[0:HEADS, 0:SEQ], wfg[:, j, :], x_t[:, j, :], start=j == 0, stop=j == KT - 1)
            last.then_inc(s_f, 1)

            for u in range(3):
                value_unit(u)
            pe.wait_ge(s_const, N_CONST)
            pe.wait_ge(s_sqsum, 1)
            for t in range(TT):
                last = nc.tensor.matmul(ssq_ps[:, t:t + 1], squares[:, 0, t * P:(t + 1) * P], ones[:, 0:1],
                                        start=True, stop=True)
            last.then_inc(s_ssq, 1)
            for u in range(3, 5):
                value_unit(u)
            pe.wait_ge(s_diag, TT)
            for t in range(TT):
                last = nc.tensor.matmul(rrow_ps[:, t * P:(t + 1) * P], ones[:, :], diag[:, t, :], start=True, stop=True)
            last.then_inc(s_rbc, 1)
            for u in range(5, V_UNITS):
                value_unit(u)

            def column_unit(dst, s, x_parts):
                last = products(dst[:, 0:SEQ], lambda a, j: w[a][:, s, j * P:(j + 1) * P],
                                lambda b, j: x_parts[b][:, j, :], KT)
                last.then_inc(s_used, 1)

            def gate_unit(s, u):
                pe.wait_ge(s_lo, u + 1)
                column_unit(bank[s % 2], s, xg)

            pe.wait_ge(s_rrow, 1)
            for s in range(RING):
                if s >= 2:
                    pe.wait_ge(s_gmul, s - 1)
                gate_unit(s, V_UNITS + s)
            with pe.Fori(V_UNITS // RING + 1, QK_0 // RING) as r:
                for s in range(RING):
                    pe.wait_ge(s_gmul, r * RING + s - V_UNITS - 1)
                    gate_unit(s, r * RING + s)

            def scores(i):
                pe.wait_ge(s_qlo, i + 1)
                pe.wait_ge(s_klo, 2 * i + 2)
                for n, (a, b) in enumerate(PASSES):
                    nc.tensor.matmul(s0_ps, q[a][:, 0:P], k[b][:, :, 0:P], start=n == 0, stop=n == 2)
                for n, (a, b) in enumerate(PASSES):
                    last = nc.tensor.matmul(s1_ps, q[a][:, P:SEQ], k[b][:, :, :], start=n == 0, stop=n == 2)
                last.then_inc(s_qk, 1)

            def transposes(i):
                pe.wait_ge(s_norm, 2 * i + 2)
                for a in range(2):
                    nc.tensor.transpose(pt0_ps[:, a, 0:P], probs[:, a, 0:P], ident[:, :])
                    nc.tensor.transpose(pt0_ps[:, a, P:SEQ], probs[:, a, P:2 * P], ident[:, :])
                    last = nc.tensor.transpose(pt1_ps[:, a, :], probs[:, a, 2 * P:3 * P], ident[:, :])
                last.then_inc(s_pt, 1)

            def values(i, b, loads):
                pe.wait_ge(s_vpair_in[b], 16 * loads)
                pe.wait_ge(s_ptlo, 2 * i + 2)
                order = [(0, PASSES[0])] + [(1, x) for x in PASSES] + [(0, x) for x in PASSES[1:]]
                for n, (t, (x, z)) in enumerate(order):
                    dst = pv_ps if t == 0 else pv_ps[:, :, P:SEQ]
                    last = nc.tensor.matmul(dst, v_pair[:, b, x * TT + t, :], (p_t0, p_t1)[t][z][:, :, :],
                                            start=n == 0, stop=n == len(order) - 1)
                last.then_inc(s_pv, 1)

            def query(i, b):
                pe.wait_ge(s_lo, QK_0 + 1 + 2 * i)
                column_unit(bank[0], 2 * b, h)

            def key(i, b):
                pe.wait_ge(s_lo, QK_0 + 2 + 2 * i)
                column_unit(bank[1], 2 * b + 1, h)

            pe.wait_ge(s_hlo, 2)
            pe.wait_ge(s_gmul, G_UNITS - 1)
            query(0, 0)
            pe.wait_ge(s_gmul, G_UNITS)
            key(0, 0)
            pe.wait_ge(s_qlo, 1)
            query(1, 1)
            scores(0)
            key(1, 1)

            def attend(i, b, loads, first=False):
                pe.wait_ge(s_qlo, i)
                query(i, b)
                pe.wait_ge(s_logits, 4 * i - 4)
                scores(i - 1)
                if not first:
                    pe.wait_ge(s_ptlo, 2 * i - 4)
                transposes(i - 2)
                key(i, b)
                if not first:
                    pe.wait_ge(s_y, 2 * i - 4)
                values(i - 2, b, loads)

            attend(2, 0, 1, first=True)
            attend(3, 1, 1)
            with pe.Fori(2, PAIRS // 2) as it:
                for b in range(2):
                    attend(2 * it + b, b, it)

            def out_part(g, pairs):
                t, c, dst = out_groups[g]
                cols = slice(c * HALF, (c + 1) * HALF)
                for p in pairs:
                    for a, b in PASSES:
                        wide = wo[b][:, p, cols] if p < OUT_OWN else w[b][:, p - OUT_OWN, cols]
                        last = nc.tensor.matmul(dst[:, :], y[a][:, p, t * P:(t + 1) * P], wide,
                                                start=p == 0 and (a, b) == PASSES[0],
                                                stop=p == PAIRS - 1 and (a, b) == PASSES[-1])
                return last

            pe.wait_ge(s_olo, OUT_OWN)
            pe.wait_ge(s_ylo, OUT_OWN)
            out_part(0, range(0, 4))
            pe.wait_ge(s_logits, 4 * PAIRS - 4)
            scores(PAIRS - 1)
            pe.wait_ge(s_ptlo, 2 * PAIRS - 4)
            transposes(PAIRS - 2)
            pe.wait_ge(s_lo, UNITS + 2)
            pe.wait_ge(s_ylo, PAIRS - 2)
            out_part(0, range(4, 6))
            pe.wait_ge(s_y, 2 * PAIRS - 4)
            values(PAIRS - 2, 0, PAIRS // 2)
            out_part(1, range(0, 6))
            pe.wait_ge(s_ptlo, 2 * PAIRS - 2)
            transposes(PAIRS - 1)
            out_part(2, range(0, 4))
            pe.wait_ge(s_y, 2 * PAIRS - 2)
            values(PAIRS - 1, 1, PAIRS // 2)
            out_part(2, range(4, 6))
            pe.wait_ge(s_logits, 4 * PAIRS)
            out_part(3, range(0, 4))
            pe.wait_ge(s_lo, UNITS + 4)
            pe.wait_ge(s_ylo, PAIRS)
            out_part(0, range(6, PAIRS)).then_inc(s_group, 1)
            out_part(1, range(6, PAIRS)).then_inc(s_group, 1)
            out_part(2, range(6, PAIRS)).then_inc(s_group, 1)
            out_part(3, range(4, PAIRS)).then_inc(s_group, 1)


def kernel(**inputs):
    import numpy as np
    import concourse.bacc as bacc
    from concourse.bass_utils import run_bass_kernel_spmd

    x = np.asarray(inputs["x"])[0]
    w_in = np.asarray(inputs["w_in"])[0]
    group = HEADS * HEAD_DIM
    names = ["qa", "ka", "va", "ga", "fa", "qb", "kb", "vb", "gb"]
    widths = [group] * 4 + [HEADS] + [group] * 4
    starts = np.cumsum([0] + widths)
    cols = {n: w_in[:, s:s + width] for n, s, width in zip(names, starts, widths)}

    def tiles(m):
        return m.reshape(KT, P, m.shape[1]).transpose(1, 0, 2)

    units = [tiles(m)[:, 2 * n:2 * n + 2].reshape(P, UNIT) for m in (cols["va"], cols["vb"]) for n in range(KT // 2)]

    def pair_unit(kind, p):
        m = cols[kind + ("a" if p < FOX_PAIRS else "b")]
        c = (p % FOX_PAIRS) * P
        return tiles(m[:, c:c + P]).reshape(P, UNIT)

    units += [pair_unit("g", p) for p in range(PAIRS)]
    for p in range(PAIRS):
        units += [pair_unit("q", p), pair_unit("k", p)]
    arrays = {
        "xt": tiles(x.T),
        "x": x.reshape(TT, P, D_MODEL).transpose(1, 0, 2),
        "g_pre": np.asarray(inputs["norm_pre_g"])[0].reshape(KT, P).T,
        "w_units": np.stack(units),
        "w_f": tiles(cols["fa"]),
        "f_bias": np.asarray(inputs["fox_forget_b"])[0].reshape(HEADS, 1),
        "w_out": np.asarray(inputs["w_out"])[0].reshape(PAIRS, P, D_MODEL),
        "g_post": np.asarray(inputs["norm_post_g"])[0].reshape(1, D_MODEL),
    }
    arrays = {n: np.ascontiguousarray(a) for n, a in arrays.items()}
    nc = bacc.Bacc("TRN2", target_bir_lowering=False, num_devices=1)
    aps = {n: nc.dram_tensor("in_" + n, a.shape, mybir.dt.from_np(a.dtype), kind="ExternalInput").ap()
           for n, a in arrays.items()}
    aps["out"] = nc.dram_tensor("out_0", (TT, P, D_MODEL), F32, kind="ExternalOutput").ap()
    hybrid_layer(nc, **aps)
    result = run_bass_kernel_spmd(nc, [{"in_" + n: a for n, a in arrays.items()}], core_ids=[0])
    return result.results[0]["out_0"].reshape(1, SEQ, D_MODEL)
```

```python
from contextlib import ExitStack

import concourse.bass as bass
from concourse import mybir

F32 = mybir.dt.float32
F32R = mybir.dt.float32r
ALU = mybir.AluOpType
ACT = mybir.ActivationFunctionType

P = 128
SEQ = 256
D_MODEL = 1024
HEAD_DIM = 64
HEADS = 8
KT = D_MODEL // P
TT = SEQ // P
PAIRS = 2 * HEADS // 2
FOX_PAIRS = HEADS // 2
HALF = D_MODEL // 2
UNIT = 1024
V_UNITS = PAIRS * P * D_MODEL // (P * UNIT)
G_UNITS, QK_UNITS = PAIRS, 2 * PAIRS
UNITS = V_UNITS + G_UNITS + QK_UNITS
QK_0 = V_UNITS + G_UNITS
RING = 4
OUT_OWN = 4
EPS = 1e-6
SCALE = HEAD_DIM ** -0.5
MASKED = -1e32
PARTS = ("hi", "lo")
X_LOADS = 4
WARM_UP = 8
N_CONST = 3
PASSES = ((0, 0), (0, 1), (1, 0))
NB = P + SEQ


def hybrid_layer(nc, xt, x, g_pre, w_units, w_f, f_bias, w_out, g_post, out):
    ctx = ExitStack()

    def sb(name, shape, dt=F32):
        return ctx.enter_context(nc.sbuf_tensor(name, shape, dt))

    def sem(name):
        return ctx.enter_context(nc.semaphore(name))

    with ctx:
        x_t = sb("x_t", [P, KT, SEQ])
        xg = [sb(f"xg_{n}", [P, KT, SEQ], F32R) for n in PARTS]
        h32 = sb("h32", [P, KT, SEQ])
        h = [sb(f"h_{n}", [P, KT, SEQ], F32R) for n in PARTS]
        squares = sb("squares", [P, KT, SEQ])
        gpre_col = sb("gpre_col", [P, KT])
        gpost_row = sb("gpost_row", [P, D_MODEL])
        wf = sb("wf", [P, KT, HEADS])
        fb_col = sb("fb_col", [HEADS, 1])
        raw = sb("raw", [P, RING, UNIT])
        w = [sb(f"w_{n}", [P, RING, UNIT], F32R) for n in PARTS]
        raw_out = sb("raw_out", [P, 2, UNIT])
        wo = [sb(f"wo_{n}", [P, OUT_OWN, D_MODEL], F32R) for n in PARTS]
        v = sb("v", [P, 2 * TT, D_MODEL], F32R)
        v_pair = sb("v_pair", [P, 2, 2 * TT, P], F32R)
        q_hi = sb("q_hi", [P, 2, SEQ], F32R)
        q_stack = sb("q_stack", [P, 2, 2, SEQ], F32R)
        k_twin = sb("k_twin", [P, 2, SEQ], F32R)
        k_lo = sb("k_lo", [P, 2, SEQ], F32R)
        bias = sb("bias", [P, 2, NB])
        logits = sb("logits", [P, 2, NB])
        probs = sb("probs", [P, 2, NB])
        p_t0 = [sb(f"p_t0_{n}", [P, 2, SEQ], F32R) for n in PARTS]
        p_t1 = [sb(f"p_t1_{n}", [P, 2, P], F32R) for n in PARTS]
        gate = sb("gate", [P, PAIRS, SEQ])
        y32 = sb("y32", [P, SEQ])
        ident = sb("ident", [P, P])
        ones = sb("ones", [P, P])
        causal = sb("causal", [P, NB])
        dist = sb("dist", [P, NB])
        slope_col = sb("slope_col", [P, HEADS])
        rrow = sb("rrow", [P, SEQ])
        ms = sb("ms", [P, TT])
        root = sb("root", [P, TT])
        rstd = sb("rstd", [P, TT])
        newton = sb("newton", [P, 2, TT])
        mx = sb("mx", [P, 4])
        neg_max = sb("neg_max", [P, 4])
        row_sum = sb("row_sum", [P, 4])
        row_inv = sb("row_inv", [P, 4])
        out_sq = sb("out_sq", [P, 5])
        y = xg
        diag = bias[:, 0, 0:SEQ].rearrange("p (t n) -> p t n", t=TT)
        decay = squares
        x_nat = x_t[:, :, :].rearrange("p a b -> p (a b)").rearrange("p (t d) -> p t d", t=TT)
        fz = logits[0:HEADS, :, :].rearrange("p a n -> p (a n)").rearrange("p (a n) -> p a n", n=SEQ)
        ones_row = probs[0:HEADS, 0, 0:SEQ]
        f_neg = probs[0:HEADS, 1, 0:SEQ]
        junk = squares[:, :, :].rearrange("p a b -> p (a b)").rearrange("p (t d) -> p t d", t=TT)
        y_post = h32[:, :, :].rearrange("p a b -> p (a b)").rearrange("p (t d) -> p t d", t=TT)
        decay_dram = nc.dram_tensor("decay_rows_scratch", (HEADS, SEQ), F32, kind="Internal").ap()

        bank = [ctx.enter_context(nc.psum_tensor(f"bank{b}", [P, HALF], F32)) for b in range(8)]
        v_banks = [[bank[2], bank[3]], [bank[4], bank[5]]]
        ssq_ps, rrow_ps, f_ps = bank[6], bank[1], bank[7]
        s0_ps = bank[2][:, 0:2 * P].rearrange("p (a n) -> p a n", a=2)
        s1_ps = bank[3][:, :].rearrange("p (a n) -> p a n", a=2)
        pt0_ps = bank[4][:, :].rearrange("p (a n) -> p a n", a=2)
        pt1_ps = bank[5][:, 0:2 * P].rearrange("p (a n) -> p a n", a=2)
        pv_ps = bank[6][:, :].rearrange("p (a n) -> p a n", a=2)
        out_groups = [(0, slice(0, HALF), bank[7][:, :]), (0, slice(HALF, D_MODEL), bank[0][:, :]),
                      (1, slice(0, HALF), bank[1][:, :]), (1, slice(HALF, HALF + SEQ), bank[2][:, 0:SEQ]),
                      (1, slice(HALF + SEQ, D_MODEL), bank[3][:, 0:SEQ])]

        head_rows = [(slice(0, HEAD_DIM), slice(HEAD_DIM, P)), (slice(HEAD_DIM, P), slice(0, HEAD_DIM))]

        s_g_in, s_wf_in, s_fb_in = sem("g_pre_in"), sem("w_f_in"), sem("f_bias_in")
        s_x_in = [sem(f"x_in{c}") for c in range(X_LOADS)]
        s_gpost_in, s_xnat_in = sem("gpost_in"), sem("x_nat_in")
        s_raw_in = [sem(f"raw_in{s}") for s in range(RING)]
        s_raw_half = sem("unit_0_first_half_in")
        s_raw_out_in = [sem(f"raw_out_in{s}") for s in range(2)]
        s_vpair_in = [sem(f"v_pair_in{s}") for s in range(2)]
        s_hi, s_lo = sem("unit_hi"), sem("unit_lo")
        s_half_hi, s_half_lo = sem("unit_0_half_hi"), sem("unit_0_half_lo")
        s_used = sem("unit_used")
        s_ohi, s_olo = sem("out_unit_hi"), sem("out_unit_lo")
        s_pool, s_dve = sem("pool_chain"), sem("dve_chain")
        s_ones, s_const = sem("ones"), sem("constants")
        s_xghi, s_xglo = sem("xg_hi"), sem("xg_lo")
        s_table = sem("activation_table")
        s_wfg, s_f = sem("wfg_ready"), sem("f_ready")
        s_sq, s_sqsum, s_ssq = sem("squares_done"), sem("square_sums"), sem("ssq_ready")
        s_ms, s_root, s_rstd = sem("mean_square"), sem("root_ready"), sem("rstd_ready")
        s_diag, s_rbc, s_rrow = sem("diag_ready"), sem("rstd_broadcast"), sem("rrow_ready")
        s_fabs, s_fexp, s_fln = sem("f_abs"), sem("f_exp"), sem("f_ln")
        s_decay, s_decay_st, s_decay_in = sem("decay_rows"), sem("decay_stored"), sem("decay_in")
        s_h32, s_hhi, s_hlo = sem("h32_ready"), sem("h_hi"), sem("h_lo")
        s_vhi, s_vlo = sem("v_hi"), sem("v_lo")
        s_gmul, s_gate = sem("gate_products"), sem("gates_ready")
        s_qhi, s_qlo = sem("q_hi"), sem("q_lo")
        s_khi, s_klo = sem("k_hi"), sem("k_lo")
        s_ktwin = sem("k_twin_ready")
        s_qk = sem("scores_ready")
        s_bias = sem("bias_ready")
        s_logits = sem("logits_ready")
        s_nmax = sem("neg_max_ready")
        s_exp = sem("exp_done")
        s_inv, s_norm = sem("row_inv_ready"), sem("probs_normed")
        s_pt = sem("probs_transposed")
        s_pthi, s_ptlo = sem("pt_hi"), sem("pt_lo")
        s_pv = sem("pv_ready")
        s_y, s_yhi, s_ylo = sem("y_ready"), sem("y_hi"), sem("y_lo")
        s_group = sem("out_group")
        s_osq, s_oms, s_oroot = sem("out_squares"), sem("out_mean_square"), sem("out_root")
        s_ypost, s_yscaled = sem("y_post_ready"), sem("y_post_scaled")
        s_fin = [[sem(f"fin_ready{t}{c}") for c in range(2)] for t in range(TT)]
        s_stored = sem("stored")

        block = ctx.enter_context(nc.Block())

        @block.sync
        def _(sp):
            n = KT // X_LOADS
            sp.dma_start(gpre_col[:, :], g_pre).then_inc(s_g_in, 16)
            for c in range(X_LOADS):
                sp.dma_start(x_t[:, n * c:n * c + n, :], xt[:, n * c:n * c + n, :]).then_inc(s_x_in[c], 16)
                if c == 0:
                    sp.dma_start(wf[:, :, :], w_f).then_inc(s_wf_in, 16)
                    sp.dma_start(raw[:, c, 0:HALF], w_units[c, :, 0:HALF]).then_inc(s_raw_half, 16)
                if c == 0:
                    sp.dma_start(raw[:, c, HALF:], w_units[c, :, HALF:]).then_inc(s_raw_in[c], 16)
                else:
                    sp.dma_start(raw[:, c, :], w_units[c]).then_inc(s_raw_in[c], 16)
            sp.dma_start(fb_col[:, :], f_bias).then_inc(s_fb_in, 16)

            def load_unit(r, s):
                sp.wait_ge(s_lo, r * RING + s + 1 - RING)
                sp.dma_start(raw[:, s, :], w_units[r * RING + s]).then_inc(s_raw_in[s], 16)

            for s in range(RING):
                load_unit(1, s)
            for u in range(V_UNITS, QK_0 + RING):
                load_unit(u // RING, u % RING)
                j = (u - V_UNITS - 3) // 2
                if u % 2 and 0 <= j < OUT_OWN:
                    if j > 1:
                        sp.wait_ge(s_olo, j - 1)
                    sp.dma_start(raw_out[:, j % 2, :], w_out[j]).then_inc(s_raw_out_in[j % 2], 16)
            sp.dma_start(gpost_row[:, :], g_post[0:1, :].to_broadcast((P, D_MODEL))).then_inc(s_gpost_in, 16)
            for s in range(RING):
                load_unit(QK_0 // RING + 1, s)
            sp.wait_ge(s_vlo, 2 * TT)
            for i in range(1, PAIRS + 1):
                if i > 2:
                    sp.wait_ge(s_pv, i - 2)
                sp.dma_start(v_pair[:, (i - 1) % 2, :, :].bitcast(F32),
                             v[:, :, (i - 1) * P:i * P].bitcast(F32)).then_inc(s_vpair_in[(i - 1) % 2], 16)
                for u in range(QK_0 + 6 + 2 * i, QK_0 + 8 + 2 * i):
                    if u < UNITS:
                        load_unit(u // RING, u % RING)
                    elif u < UNITS + RING:
                        sp.wait_ge(s_lo, u + 1 - RING)
                        sp.dma_start(raw[:, u % RING, :], w_out[OUT_OWN + u - UNITS]).then_inc(s_raw_in[u % RING], 16)
            sp.wait_ge(s_h32, KT)
            sp.dma_start(x_nat, x).then_inc(s_xnat_in, 16)
            for t, c in ((0, 0), (0, 1), (1, 0)):
                sp.wait_ge(s_fin[t][c], 1)
                sp.dma_start(out[t, :, c * HALF:(c + 1) * HALF],
                             x_nat[:, t, c * HALF:(c + 1) * HALF]).then_inc(s_stored, 16)
            sp.wait_ge(s_stored, 16 * 2 * TT)

        @block.gpsimd
        def _(pool):
            done = [0]

            def link(ins):
                done[0] += 1
                ins.then_inc(s_pool, 1)
                pool.wait_ge(s_pool, done[0])

            pool.memset(ones[:, :], 1.0).then_inc(s_ones, 1)
            link(pool.memset(ident[:, :], 0.0))
            pool.affine_select(out=ident[:, :], in_=ident[:, :], compare_op=ALU.not_equal, fill=1.0,
                               base=0, pattern=[[-1, P]], channel_multiplier=1).then_inc(s_const, 1)
            pool.memset(k_lo[:, :, :].bitcast(F32), 0.0).then_inc(s_const, 1)
            pool.memset(ones_row, 1.0).then_inc(s_const, 1)
            pool.memset(causal[:, :], 0.0).then_inc(s_pool, 1)
            pool.iota(dist[:, 0:P], pattern=[[1, P]], base=0, channel_multiplier=-1,
                      allow_small_or_imprecise_dtypes=True).then_inc(s_pool, 1)
            pool.iota(dist[:, P:NB], pattern=[[1, SEQ]], base=-P, channel_multiplier=-1,
                      allow_small_or_imprecise_dtypes=True).then_inc(s_pool, 1)
            for n in range(HEADS):
                pool.memset(slope_col[:, n:n + 1], 2.0 ** (-8.0 * (n + 1) / HEADS) / SCALE).then_inc(s_pool, 1)
            done[0] += 3 + HEADS
            pool.wait_ge(s_pool, done[0])
            for m in (causal, dist):
                for lo, hi, base in ((0, P, 0), (P, NB, P)):
                    pool.affine_select(out=m[:, lo:hi], in_=m[:, lo:hi], compare_op=ALU.is_ge, fill=MASKED,
                                       base=base, pattern=[[-1, hi - lo]], channel_multiplier=1).then_inc(s_pool, 1)
                    done[0] += 1

            n = KT // X_LOADS
            for c in range(1, X_LOADS):
                pool.wait_ge(s_sq, c + 1)
                link(pool.tensor_tensor(squares[:, 0:n, :], squares[:, 0:n, :], squares[:, n * c:n * c + n, :], ALU.add))
            pool.tensor_tensor(squares[:, 0, :], squares[:, 0, :], squares[:, 1, :], ALU.add).then_inc(s_sqsum, 1)

            def fox_bias(i):
                for lo, hi in ((0, P), (P, NB)):
                    last = pool.tensor_tensor(bias[:, :, lo:hi], decay[:, bass.ds(2 * i, 2), 0:hi - lo],
                                              causal[:, lo:hi].unsqueeze(1).to_broadcast((P, 2, hi - lo)), ALU.add)
                    if lo == 0:
                        last.then_inc(s_bias, 1)
                last.then_inc(s_bias, 1)

            def moba_bias(i):
                for lo, hi in ((0, P), (P, NB)):
                    pool.tensor_tensor(bias[:, :, lo:hi],
                                       dist[:, lo:hi].unsqueeze(1).to_broadcast((P, 2, hi - lo)),
                                       slope_col[:, bass.ds(2 * i - HEADS, 2)].unsqueeze(2).to_broadcast((P, 2, hi - lo)),
                                       ALU.mult).then_inc(s_bias, 1)

            def norm_probs(i):
                pool.wait_ge(s_inv, i + 1)
                for t, (lo, hi) in enumerate(((0, P), (P, NB))):
                    pool.tensor_tensor(probs[:, :, lo:hi], probs[:, :, lo:hi],
                                       row_inv[:, t::2].unsqueeze(2).to_broadcast((P, 2, hi - lo)),
                                       ALU.mult).then_inc(s_norm, 1)

            def y_low(i):
                pool.wait_ge(s_yhi, i + 1)
                pool.tensor_tensor(y[1][:, bass.ds(i, 1), :], y32[:, :].unsqueeze(1),
                                   y[0][:, bass.ds(i, 1), :].bitcast(F32), ALU.subtract).then_inc(s_ylo, 1)

            def out_unit_low(j):
                pool.wait_ge(s_ohi, j + 1)
                pool.tensor_tensor(wo[1][:, j, :], raw_out[:, j % 2, :], wo[0][:, j, :].bitcast(F32),
                                   ALU.subtract).then_inc(s_olo, 1)

            for j in range(OUT_OWN - 1):
                out_unit_low(j)
            pool.wait_ge(s_pool, done[0])
            pool.wait_ge(s_decay_in, 16)
            fox_bias(0)
            out_unit_low(OUT_OWN - 1)
            pool.wait_ge(s_logits, 4)
            norm_probs(0)
            fox_bias(1)
            with pool.Fori(2, FOX_PAIRS) as i:
                norm_probs(i - 1)
                pool.wait_ge(s_logits, 4 * i)
                fox_bias(i)
                y_low(i - 2)
            with pool.Fori(FOX_PAIRS, PAIRS) as i:
                norm_probs(i - 1)
                pool.wait_ge(s_logits, 4 * i)
                moba_bias(i)
                y_low(i - 2)
            norm_probs(PAIRS - 1)
            y_low(PAIRS - 2)
            y_low(PAIRS - 1)
            pool.wait_ge(s_xnat_in, 16)
            pool.wait_ge(s_ypost, 2)
            pool.wait_ge(s_rstd, 2)
            pool.tensor_tensor(y_post[:, 0, HALF:], y_post[:, 0, HALF:], rstd[:, 0:1].to_broadcast((P, HALF)),
                               ALU.mult).then_inc(s_yscaled, 1)
            pool.wait_ge(s_yscaled, 1)
            pool.tensor_tensor(x_nat[:, 0, HALF:], x_nat[:, 0, HALF:], y_post[:, 0, HALF:], ALU.add).then_inc(s_fin[0][1], 1)

        @block.scalar
        def _(act):
            def unit_high(s, n, used=None):
                act.wait_ge(s_raw_in[s], n)
                if used is not None:
                    act.wait_ge(s_used, used)
                nc.scalar.activation(w[0][:, s, :], raw[:, s, :], ACT.Copy).then_inc(s_hi, 1)

            def out_unit_high(j):
                act.wait_ge(s_raw_out_in[j % 2], 16 * (j // 2 + 1))
                nc.scalar.activation(wo[0][:, j, :], raw_out[:, j % 2, :], ACT.Copy).then_inc(s_ohi, 1)

            act.wait_ge(s_ones, 1)
            nc.scalar.activation(root[:, 0:1], ones[:, 0:1], ACT.Copy).then_inc(s_table, 1)
            act.wait_ge(s_g_in, 16)
            n = KT // X_LOADS

            def square(c):
                nc.scalar.activation(squares[:, n * c:n * c + n, :], x_t[:, n * c:n * c + n, :],
                                     ACT.Square).then_inc(s_sq, 1)

            for c in range(X_LOADS):
                act.wait_ge(s_x_in[c], 16)
                for j in range(n * c, n * c + n):
                    nc.scalar.activation(xg[0][:, j, :], x_t[:, j, :], ACT.Copy,
                                         scale=gpre_col[:, j:j + 1]).then_inc(s_xghi, 1)
                if c == 0:
                    act.wait_ge(s_raw_half, 16)
                    nc.scalar.activation(w[0][:, 0, 0:HALF], raw[:, 0, 0:HALF], ACT.Copy).then_inc(s_half_hi, 1)
                    act.wait_ge(s_raw_in[0], 16)
                    nc.scalar.activation(w[0][:, 0, HALF:], raw[:, 0, HALF:], ACT.Copy).then_inc(s_hi, 1)
                else:
                    unit_high(c, 16)
                    square(c - 1)
            square(X_LOADS - 1)
            unit_high(0, 32, 1)
            unit_high(1, 32, 2)
            unit_high(2, 32, 3)
            act.wait_ge(s_ms, 1)
            act.wait_ge(s_table, 1)
            nc.scalar.activation(root[:, :], ms[:, :], ACT.Sqrt).then_inc(s_root, 1)

            def value_high(c):
                act.wait_ge(s_used, 4 * c + 4)
                act.wait_ge(s_rstd, 1)
                for t in range(TT):
                    nc.scalar.activation(v[:, t, c * HALF:(c + 1) * HALF], v_banks[c][t][:, :], ACT.Copy,
                                         scale=rstd[:, t:t + 1]).then_inc(s_vhi, 1)

            unit_high(3, 32, 4)
            value_high(0)
            unit_high(0, 48, 5)
            act.wait_ge(s_fabs, 1)
            nc.scalar.activation(fz[:, 1, :], fz[:, 1, :], ACT.Exp, scale=-1.0).then_inc(s_fexp, 1)
            act.wait_ge(s_fexp, 1)
            nc.scalar.activation(fz[:, 2, :], fz[:, 1, :], ACT.Ln, bias=1.0).then_inc(s_fln, 1)
            unit_high(1, 48, 6)
            value_high(1)

            def gate_round(r):
                for s in range(RING):
                    unit_high((s + 2) % RING, 16 * (r + 1 + (s + 2) // RING), r * RING + s - 1)
                    if r == V_UNITS // RING and s == 0:
                        act.wait_ge(s_decay, 1)
                        act.dma_start(decay_dram, fz[:, 0, :]).then_inc(s_decay_st, 16)
                    if r > V_UNITS // RING and s % 2 == 0:
                        part = slice(s // 2 * KT // 2, (s // 2 + 1) * KT // 2)
                        act.wait_ge(s_h32, (s // 2 + 1) * KT // 2)
                        nc.scalar.activation(h[0][:, part, :], h32[:, part, :], ACT.Copy).then_inc(s_hhi, 1)
                    if s % 2:
                        out_unit_high(r * 2 - V_UNITS // 2 + s // 2)

            gate_round(V_UNITS // RING)
            act.wait_ge(s_decay_st, 16)
            act.dma_start(decay[:, :, :], decay_dram.partition_broadcast(P)).then_inc(s_decay_in, 16)
            gate_round(V_UNITS // RING + 1)

            def probs_high(i):
                act.wait_ge(s_pt, i + 1)
                nc.scalar.activation(p_t0[0][:, :, :], pt0_ps, ACT.Copy).then_inc(s_pthi, 1)
                nc.scalar.activation(p_t1[0][:, :, :], pt1_ps, ACT.Copy).then_inc(s_pthi, 1)

            def exps(i):
                for a in range(2):
                    act.wait_ge(s_nmax, 2 * i + a + 1)
                    for t, (lo, hi) in enumerate(((0, P), (P, NB))):
                        c = 2 * a + t
                        nc.scalar.activation(probs[:, a, lo:hi], logits[:, a, lo:hi], ACT.Exp,
                                             bias=neg_max[:, c:c + 1], scale=SCALE,
                                             accum_out=row_sum[:, c:c + 1]).then_inc(s_exp, 1)

            def y_high(i):
                act.wait_ge(s_y, 2 * i + 2)
                nc.scalar.activation(y[0][:, bass.ds(i, 1), :], y32[:, :].unsqueeze(1), ACT.Copy).then_inc(s_yhi, 1)

            def query_high(i, b):
                act.wait_ge(s_used, QK_0 + 1 + 2 * i)
                nc.scalar.activation(q_hi[:, b, :], bank[0][:, 0:SEQ], ACT.Copy).then_inc(s_qhi, 1)

            def query_stack(i, b):
                act.wait_ge(s_qhi, 3 * i + 1)
                for a, (own, other) in enumerate(head_rows):
                    nc.scalar.activation(q_stack[own, b, a, :], q_hi[own, b, :], ACT.Copy).then_inc(s_qhi, 1)

            def key_high(i):
                act.wait_ge(s_used, QK_0 + 2 + 2 * i)
                for a, (own, other) in enumerate(head_rows):
                    nc.scalar.activation(k_twin[own, a, :], bank[1][own, 0:SEQ], ACT.Copy).then_inc(s_khi, 1)

            def key_twin(i):
                act.wait_ge(s_khi, 2 * i + 2)
                for a, (own, other) in enumerate(head_rows):
                    nc.scalar.activation(k_twin[other, a, :], k_twin[own, a, :].bitcast(F32),
                                         ACT.Copy).then_inc(s_ktwin, 1)

            def gates_silu():
                act.wait_ge(s_gmul, PAIRS)
                nc.scalar.activation(gate[:, :, :], gate[:, :, :], ACT.Silu).then_inc(s_gate, 1)

            def attend(i, b, n, first=0, fresh=False):
                unit_high((2 * b + 2) % RING, n, 2 * i + QK_0 - 1)
                if first != 1:
                    key_twin(i - 1)
                if first == 0 and not fresh:
                    y_high(i - 3)
                if first == 1:
                    gates_silu()
                query_high(i, b)
                if first == 0:
                    probs_high(i - 2)
                query_stack(i, b)
                if first != 2:
                    unit_high((2 * b + 3) % RING, n, 2 * i + QK_0)
                if first != 1:
                    exps(i - 1)
                if first == 2:
                    unit_high((2 * b + 3) % RING, n, 2 * i + QK_0)
                key_high(i)

            act.wait_ge(s_const, N_CONST)
            attend(0, 0, 16 * (QK_0 // RING + 1), first=1)
            attend(1, 1, 16 * (QK_0 // RING + 2), first=2)
            attend(2, 0, 16 * (QK_0 // RING + 2), fresh=True)
            attend(3, 1, 16 * (QK_0 // RING + 3))
            with act.Fori(2, PAIRS // 2) as it:
                for b in range(2):
                    attend(2 * it + b, b, 16 * (it + QK_0 // RING + 1 + b))
            unit_high(2, 16 * (UNITS // RING + 1), UNITS - 1)
            key_twin(PAIRS - 1)
            y_high(PAIRS - 3)
            probs_high(PAIRS - 2)
            unit_high(3, 16 * (UNITS // RING + 1), UNITS)
            exps(PAIRS - 1)
            y_high(PAIRS - 2)
            probs_high(PAIRS - 1)
            y_high(PAIRS - 1)
            nc.scalar.activation(junk[:, 0, 0:1], rstd[:, 0:1], ACT.Sqrt).then_inc(s_table, 1)
            act.wait_ge(s_table, 2)
            for n, (t, cols, group) in enumerate(out_groups):
                act.wait_ge(s_group, n + 1)
                nc.scalar.activation(junk[:, t, cols], group, ACT.Square, accum_out=out_sq[:, n:n + 1]).then_inc(s_osq, 1)
                if cols.stop == D_MODEL:
                    act.wait_ge(s_oms, t + 1)
                    nc.scalar.activation(root[:, t:t + 1], ms[:, t:t + 1], ACT.Sqrt).then_inc(s_oroot, 1)
            act.wait_ge(s_fin[TT - 1][1], 1)
            act.dma_start(out[TT - 1, :, HALF:], x_nat[:, TT - 1, HALF:]).then_inc(s_stored, 16)

        @block.vector
        def _(dve):
            done = [0]

            def link(ins):
                done[0] += 1
                ins.then_inc(s_dve, 1)
                dve.wait_ge(s_dve, done[0])

            def unit_low(s, count):
                dve.wait_ge(s_hi, count)
                nc.vector.tensor_tensor(w[1][:, s, :], raw[:, s, :], w[0][:, s, :].bitcast(F32),
                                        ALU.subtract).then_inc(s_lo, 1)

            dve.wait_ge(s_g_in, 16)
            dve.wait_ge(s_wf_in, 16)
            nc.vector.tensor_tensor(wf[:, :, :], wf[:, :, :],
                                    gpre_col[:, :].unsqueeze(2).to_broadcast((P, KT, HEADS)), ALU.mult).then_inc(s_wfg, 1)
            for j in range(KT):
                if j == KT // X_LOADS:
                    dve.wait_ge(s_half_hi, 1)
                    nc.vector.tensor_tensor(w[1][:, 0, 0:HALF], raw[:, 0, 0:HALF], w[0][:, 0, 0:HALF].bitcast(F32),
                                            ALU.subtract).then_inc(s_half_lo, 1)
                    dve.wait_ge(s_hi, 1)
                    nc.vector.tensor_tensor(w[1][:, 0, HALF:], raw[:, 0, HALF:], w[0][:, 0, HALF:].bitcast(F32),
                                            ALU.subtract).then_inc(s_lo, 1)
                elif j and j % (KT // X_LOADS) == 0:
                    unit_low(j // (KT // X_LOADS) - 1, j // (KT // X_LOADS))
                dve.wait_ge(s_xghi, j + 1)
                nc.vector.scalar_tensor_tensor(out=xg[1][:, j, :], in0=x_t[:, j, :], scalar=gpre_col[:, j:j + 1],
                                               in1=xg[0][:, j, :].bitcast(F32), op0=ALU.mult,
                                               op1=ALU.subtract).then_inc(s_xglo, 1)
            for u in range(X_LOADS - 1, 7):
                unit_low(u % RING, u + 1)

            dve.wait_ge(s_ssq, 1)
            nc.vector.tensor_scalar(ms[:, :], ssq_ps[:, 0:TT], 1.0 / D_MODEL, EPS, ALU.mult, ALU.add).then_inc(s_ms, 1)
            dve.wait_ge(s_root, 1)
            inv, step = newton[:, 0, :], newton[:, 1, :]
            link(nc.vector.reciprocal(inv, root[:, :]))
            link(nc.vector.tensor_tensor(step, inv, inv, ALU.mult))
            link(nc.vector.tensor_tensor(step, step, ms[:, :], ALU.mult))
            link(nc.vector.tensor_scalar(step, step, -0.5, 1.5, ALU.mult, ALU.add))
            nc.vector.tensor_tensor(rstd[:, :], inv, step, ALU.mult).then_inc(s_rstd, 1)
            dve.wait_ge(s_rstd, 1)
            dve.wait_ge(s_const, N_CONST)
            for t in range(TT):
                nc.vector.tensor_scalar(diag[:, t, :], ident[:, :], rstd[:, t:t + 1], None, ALU.mult).then_inc(s_diag, 1)
            unit_low(3, 8)

            def value_low(c):
                for t in range(TT):
                    dve.wait_ge(s_vhi, 2 * c + t + 1)
                    cols = slice(c * HALF, (c + 1) * HALF)
                    nc.vector.scalar_tensor_tensor(out=v[:, TT + t, cols], in0=v_banks[c][t][:, :],
                                                   scalar=rstd[:, t:t + 1], in1=v[:, t, cols].bitcast(F32),
                                                   op0=ALU.mult, op1=ALU.subtract).then_inc(s_vlo, 1)

            dve.wait_ge(s_rbc, 1)
            nc.vector.tensor_copy(rrow[:, :], rrow_ps[:, 0:SEQ]).then_inc(s_rrow, 1)
            dve.wait_ge(s_rrow, 1)
            dve.wait_ge(s_f, 1)
            dve.wait_ge(s_fb_in, 16)
            link(nc.vector.tensor_tensor(fz[:, 0, :], f_ps[0:HEADS, 0:SEQ], rrow[0:HEADS, :], ALU.mult))
            link(nc.vector.tensor_scalar(fz[:, 0, :], fz[:, 0, :], fb_col[:, :], None, ALU.add))
            link(nc.vector.tensor_scalar(fz[:, 1, :], fz[:, 0, :], -1.0, None, ALU.mult))
            nc.vector.tensor_tensor(fz[:, 1, :], fz[:, 1, :], fz[:, 0, :], ALU.max).then_inc(s_fabs, 1)
            link(nc.vector.tensor_scalar(f_neg, fz[:, 0, :], 0.0, 1.0 / SCALE, ALU.min, ALU.mult))
            unit_low(0, 9)
            value_low(0)
            unit_low(1, 10)
            dve.wait_ge(s_fln, 1)
            link(nc.vector.scalar_tensor_tensor(out=fz[:, 1, :], in0=fz[:, 2, :], scalar=1.0 / SCALE, in1=f_neg,
                                                op0=ALU.mult, op1=ALU.subtract))
            nc.vector.tensor_tensor_scan(fz[:, 0, :], ones_row, fz[:, 1, :], 0.0, ALU.mult, ALU.add).then_inc(s_decay, 1)
            value_low(1)

            def gate_round(r):
                for s in range(RING):
                    unit_low((s + 2) % RING, r * RING + s + 3)
                    u = r * RING + s
                    dve.wait_ge(s_used, u + 1)
                    nc.vector.tensor_tensor(gate[:, u - V_UNITS, :], bank[s % 2][:, 0:SEQ], rrow[:, :],
                                            ALU.mult).then_inc(s_gmul, 1)
                    if r == V_UNITS // RING:
                        for j in (2 * s, 2 * s + 1):
                            nc.vector.scalar_tensor_tensor(out=h32[:, j, :], in0=x_t[:, j, :],
                                                           scalar=gpre_col[:, j:j + 1], in1=rrow[:, :],
                                                           op0=ALU.mult, op1=ALU.mult).then_inc(s_h32, 1)
                    if r > V_UNITS // RING and s % 2 == 0:
                        dve.wait_ge(s_hhi, s // 2 + 1)
                        part = slice(s // 2 * KT // 2, (s // 2 + 1) * KT // 2)
                        nc.vector.tensor_tensor(h[1][:, part, :], h32[:, part, :], h[0][:, part, :].bitcast(F32),
                                                ALU.subtract).then_inc(s_hlo, 1)

            gate_round(V_UNITS // RING)
            gate_round(V_UNITS // RING + 1)

            def scores_there(i):
                dve.wait_ge(s_qk, i + 1)
                dve.wait_ge(s_bias, 2 * i + 2)

            def probs_low(i, scored=None):
                for n, (dst, src) in enumerate(((p_t0, pt0_ps), (p_t1, pt1_ps))):
                    dve.wait_ge(s_pthi, 2 * i + n + 1)
                    if n and scored is not None:
                        scores_there(scored)
                    nc.vector.tensor_tensor(dst[1][:, :, :], src, dst[0][:, :, :].bitcast(F32),
                                            ALU.subtract).then_inc(s_ptlo, 1)

            def row_logits(i, a):
                for t, (lo, hi, ps) in enumerate(((0, P, s0_ps), (P, NB, s1_ps))):
                    c = 2 * a + t
                    nc.vector.tensor_tensor_reduce(out=logits[:, a, lo:hi], in0=ps[:, a, :], in1=bias[:, a, lo:hi],
                                                   scale=1.0, scalar=-3.0e38, op0=ALU.add, op1=ALU.max,
                                                   accum_out=mx[:, c:c + 1]).then_inc(s_logits, 1)
                dve.wait_ge(s_logits, 4 * i + 2 * a + 2)
                nc.vector.tensor_scalar(neg_max[:, 2 * a:2 * a + 2], mx[:, 2 * a:2 * a + 2], -SCALE, None,
                                        ALU.mult).then_inc(s_nmax, 1)

            def row_inverses(i):
                dve.wait_ge(s_exp, 4 * i + 4)
                nc.vector.reciprocal(row_inv[:, :], row_sum[:, :]).then_inc(s_inv, 1)

            def query_low(i, b):
                dve.wait_ge(s_qhi, 3 * i + 1)
                for a, (own, other) in enumerate(head_rows):
                    nc.vector.tensor_tensor(q_stack[other, b, a, :], bank[0][own, 0:SEQ], q_hi[own, b, :].bitcast(F32),
                                            ALU.subtract).then_inc(s_qlo, 1)

            def key_low(i):
                dve.wait_ge(s_khi, 2 * i + 2)
                for a, (own, other) in enumerate(head_rows):
                    nc.vector.tensor_tensor(k_lo[own, a, :], bank[1][own, 0:SEQ], k_twin[own, a, :].bitcast(F32),
                                            ALU.subtract).then_inc(s_klo, 1)

            def gated(i):
                dve.wait_ge(s_pv, i + 1)
                for a in range(2):
                    rows = slice(a * HEAD_DIM, (a + 1) * HEAD_DIM)
                    nc.vector.tensor_tensor(y32[rows, :].unsqueeze(1), pv_ps[rows, a:a + 1, :],
                                            gate[rows, bass.ds(i, 1), :], ALU.mult).then_inc(s_y, 1)

            def attend(i, b, first=0):
                unit_low((2 * b + 2) % RING, QK_0 + 3 + 2 * i)
                if first == 0 and not (isinstance(i, int) and i == 2):
                    dve.wait_ge(s_norm, 2 * i - 2)
                if first == 2:
                    scores_there(i - 1)
                query_low(i, b)
                if first == 0:
                    probs_low(i - 2, i - 1)
                if first != 1:
                    row_logits(i - 1, 0)
                    row_logits(i - 1, 1)
                if first != 2:
                    unit_low((2 * b + 3) % RING, QK_0 + 4 + 2 * i)
                if first != 1:
                    row_inverses(i - 1)
                if first == 2:
                    unit_low((2 * b + 3) % RING, QK_0 + 4 + 2 * i)
                key_low(i)
                if first == 0:
                    if not (isinstance(i, int) and i == 2):
                        dve.wait_ge(s_ylo, i - 2)
                    gated(i - 2)

            attend(0, 0, first=1)
            attend(1, 1, first=2)
            dve.wait_ge(s_gate, 1)
            attend(2, 0)
            attend(3, 1)
            with dve.Fori(2, PAIRS // 2) as it:
                for b in range(2):
                    attend(2 * it + b, b)
            unit_low(2, UNITS + 3)
            probs_low(PAIRS - 2, PAIRS - 1)
            row_logits(PAIRS - 1, 0)
            row_logits(PAIRS - 1, 1)
            unit_low(3, UNITS + 4)
            row_inverses(PAIRS - 1)
            dve.wait_ge(s_ylo, PAIRS - 2)
            gated(PAIRS - 2)
            probs_low(PAIRS - 1)
            dve.wait_ge(s_ylo, PAIRS - 1)
            gated(PAIRS - 1)

            dve.wait_ge(s_gpost_in, 16)
            dve.wait_ge(s_xnat_in, 16)

            def times_g(n):
                t, cols, group = out_groups[n]
                dve.wait_ge(s_osq, n + 1)
                nc.vector.tensor_tensor(y_post[:, t, cols], group, gpost_row[:, cols], ALU.mult).then_inc(s_ypost, 1)

            def out_rstd(t, groups):
                r, a, m = newton[:, 0, t:t + 1], newton[:, 1, t:t + 1], ms[:, t:t + 1]
                for n in groups:
                    dve.wait_ge(s_osq, n + 1)
                    if n == groups[0]:
                        ins = nc.vector.tensor_scalar(m, out_sq[:, n:n + 1], 1.0 / D_MODEL, EPS, ALU.mult, ALU.add)
                    else:
                        ins = nc.vector.scalar_tensor_tensor(out=m, in0=out_sq[:, n:n + 1], scalar=1.0 / D_MODEL,
                                                             in1=m, op0=ALU.mult, op1=ALU.add)
                    if n != groups[-1]:
                        link(ins)
                ins.then_inc(s_oms, 1)
                times_g(groups[-1])
                dve.wait_ge(s_oms, t + 1)
                link(nc.vector.tensor_scalar(a, m, -0.5, None, ALU.mult))
                dve.wait_ge(s_oroot, t + 1)
                link(nc.vector.reciprocal(r, root[:, t:t + 1]))
                link(nc.vector.scalar_tensor_tensor(out=a, in0=r, scalar=a, in1=r, op0=ALU.mult, op1=ALU.mult))
                nc.vector.scalar_tensor_tensor(out=rstd[:, t:t + 1], in0=a, scalar=1.5, in1=r, op0=ALU.add,
                                               op1=ALU.mult).then_inc(s_rstd, 1)
                dve.wait_ge(s_rstd, t + 2)

            def residual(t, c, groups):
                dve.wait_ge(s_ypost, groups)
                cols = slice(c * HALF, (c + 1) * HALF)
                nc.vector.scalar_tensor_tensor(out=x_nat[:, t, cols], in0=y_post[:, t, cols], scalar=rstd[:, t:t + 1],
                                               in1=x_nat[:, t, cols], op0=ALU.mult, op1=ALU.add).then_inc(s_fin[t][c], 1)

            times_g(0)
            out_rstd(0, (0, 1))
            times_g(2)
            residual(0, 0, 1)
            times_g(3)
            out_rstd(1, (2, 3, 4))
            residual(1, 0, 3)
            residual(1, 1, 5)

        @block.tensor
        def _(pe):
            def products(dst, stationary, moving, count):
                n = 0
                for j in range(count):
                    for a, b in PASSES:
                        n += 1
                        last = nc.tensor.matmul(dst, stationary(a, j), moving(b, j), start=n == 1,
                                                stop=n == count * len(PASSES))
                return last

            def value_half(u, n):
                c, m = divmod(u, V_UNITS // 2)
                j = 2 * m + n
                if u == 0 and n == 0:
                    pe.wait_ge(s_half_lo, 1)
                else:
                    pe.wait_ge(s_lo, u + 1)
                if c == 0:
                    pe.wait_ge(s_xglo, j + 1)
                for a, b in PASSES:
                    for t in range(TT):
                        last = nc.tensor.matmul(v_banks[c][t][:, :], xg[a][:, j, t * P:(t + 1) * P],
                                                w[b][:, u % RING, n * HALF:(n + 1) * HALF],
                                                start=j == 0 and (a, b) == PASSES[0],
                                                stop=j == KT - 1 and (a, b) == PASSES[-1])
                return last

            def value_unit(u):
                value_half(u, 0)
                value_half(u, 1).then_inc(s_used, 1)

            def forget(c):
                pe.wait_ge(s_x_in[c], 16)
                for j in range(c * KT // X_LOADS, (c + 1) * KT // X_LOADS):
                    last = nc.tensor.matmul(f_ps[0:HEADS, 0:SEQ], wf[:, j, :], x_t[:, j, :], start=j == 0, stop=j == KT - 1)
                return last

            pe.wait_ge(s_ones, 1)
            for n in range(WARM_UP):
                nc.tensor.matmul(ssq_ps[:, 0:P], ones[:, :], ones[:, :], start=True, stop=True)
            pe.wait_ge(s_wfg, 1)
            forget(0)
            value_half(0, 0)
            forget(1)
            value_half(0, 1).then_inc(s_used, 1)
            value_unit(1)
            forget(2)
            value_unit(2)
            forget(3).then_inc(s_f, 1)
            value_unit(3)
            pe.wait_ge(s_sqsum, 1)
            for t in range(TT):
                last = nc.tensor.matmul(ssq_ps[:, t:t + 1], squares[:, 0, t * P:(t + 1) * P], ones[:, 0:1],
                                        start=True, stop=True)
            last.then_inc(s_ssq, 1)
            for u in range(4, 6):
                value_unit(u)
            pe.wait_ge(s_diag, TT)
            for t in range(TT):
                last = nc.tensor.matmul(rrow_ps[:, t * P:(t + 1) * P], ones[:, :], diag[:, t, :], start=True, stop=True)
            last.then_inc(s_rbc, 1)
            for u in range(6, V_UNITS):
                value_unit(u)

            def column_unit(dst, s, x_parts):
                last = products(dst[:, 0:SEQ], lambda a, j: w[a][:, s, j * P:(j + 1) * P],
                                lambda b, j: x_parts[b][:, j, :], KT)
                last.then_inc(s_used, 1)

            def gate_unit(s, u):
                pe.wait_ge(s_lo, u + 1)
                column_unit(bank[s % 2], s, xg)

            pe.wait_ge(s_rrow, 1)
            for s in range(RING):
                if s >= 2:
                    pe.wait_ge(s_gmul, s - 1)
                gate_unit(s, V_UNITS + s)
            with pe.Fori(V_UNITS // RING + 1, QK_0 // RING) as r:
                for s in range(RING):
                    pe.wait_ge(s_gmul, r * RING + s - V_UNITS - 1)
                    gate_unit(s, r * RING + s)

            def scores(i, b):
                pe.wait_ge(s_qhi, 3 * i + 3)
                pe.wait_ge(s_qlo, 2 * i + 2)
                pe.wait_ge(s_ktwin, 2 * i + 2)
                pe.wait_ge(s_klo, 2 * i + 2)
                for dst, rows, keys in ((s0_ps, slice(0, P), P), (s1_ps, slice(P, SEQ), SEQ)):
                    nc.tensor.matmul(dst, q_hi[:, b, rows], k_lo[:, :, 0:keys], start=True, stop=False)
                    for a in range(2):
                        last = nc.tensor.matmul(dst[:, a, :], q_stack[:, b, a, rows], k_twin[:, a, 0:keys],
                                                start=False, stop=a == 1)
                last.then_inc(s_qk, 1)

            def transposes(i):
                pe.wait_ge(s_norm, 2 * i + 2)
                for a in range(2):
                    nc.tensor.transpose(pt0_ps[:, a, 0:P], probs[:, a, 0:P], ident[:, :])
                    nc.tensor.transpose(pt0_ps[:, a, P:SEQ], probs[:, a, P:2 * P], ident[:, :])
                    last = nc.tensor.transpose(pt1_ps[:, a, :], probs[:, a, 2 * P:3 * P], ident[:, :])
                last.then_inc(s_pt, 1)

            def values(i, b, loads):
                pe.wait_ge(s_vpair_in[b], 16 * loads)
                pe.wait_ge(s_ptlo, 2 * i + 2)
                order = [(0, PASSES[0])] + [(1, x) for x in PASSES] + [(0, x) for x in PASSES[1:]]
                for n, (t, (x, z)) in enumerate(order):
                    dst = pv_ps if t == 0 else pv_ps[:, :, P:SEQ]
                    last = nc.tensor.matmul(dst, v_pair[:, b, x * TT + t, :], (p_t0, p_t1)[t][z][:, :, :],
                                            start=n == 0, stop=n == len(order) - 1)
                last.then_inc(s_pv, 1)

            def query(i, b):
                pe.wait_ge(s_lo, QK_0 + 1 + 2 * i)
                column_unit(bank[0], 2 * b, h)

            def key(i, b):
                pe.wait_ge(s_lo, QK_0 + 2 + 2 * i)
                column_unit(bank[1], 2 * b + 1, h)

            pe.wait_ge(s_hlo, 2)
            pe.wait_ge(s_gmul, G_UNITS - 1)
            query(0, 0)
            pe.wait_ge(s_gmul, G_UNITS)
            key(0, 0)
            pe.wait_ge(s_qlo, 2)
            query(1, 1)
            scores(0, 0)
            key(1, 1)

            def attend(i, b, loads, first=False):
                pe.wait_ge(s_qlo, 2 * i)
                query(i, b)
                if not first:
                    pe.wait_ge(s_ptlo, 2 * i - 4)
                transposes(i - 2)
                pe.wait_ge(s_logits, 4 * i - 4)
                scores(i - 1, 1 - b)
                key(i, b)
                if not first:
                    pe.wait_ge(s_y, 2 * i - 4)
                values(i - 2, b, loads)

            attend(2, 0, 1, first=True)
            attend(3, 1, 1)
            with pe.Fori(2, PAIRS // 2) as it:
                for b in range(2):
                    attend(2 * it + b, b, it)

            def out_part(g, pairs):
                t, cols, dst = out_groups[g]
                for p in pairs:
                    for a, b in PASSES:
                        wide = wo[b][:, p, cols] if p < OUT_OWN else w[b][:, p - OUT_OWN, cols]
                        last = nc.tensor.matmul(dst, y[a][:, p, t * P:(t + 1) * P], wide,
                                                start=p == 0 and (a, b) == PASSES[0],
                                                stop=p == PAIRS - 1 and (a, b) == PASSES[-1])
                return last

            pe.wait_ge(s_olo, OUT_OWN)
            pe.wait_ge(s_ylo, OUT_OWN)
            out_part(0, range(0, 4))
            pe.wait_ge(s_ptlo, 2 * PAIRS - 4)
            transposes(PAIRS - 2)
            pe.wait_ge(s_logits, 4 * PAIRS - 4)
            scores(PAIRS - 1, 1)
            out_part(1, range(0, 2))
            pe.wait_ge(s_lo, UNITS + 2)
            pe.wait_ge(s_ylo, PAIRS - 2)
            out_part(0, range(4, 6))
            pe.wait_ge(s_y, 2 * PAIRS - 4)
            values(PAIRS - 2, 0, PAIRS // 2)
            out_part(1, range(2, 6))
            pe.wait_ge(s_ptlo, 2 * PAIRS - 2)
            transposes(PAIRS - 1)
            out_part(2, range(0, 4))
            pe.wait_ge(s_y, 2 * PAIRS - 2)
            values(PAIRS - 1, 1, PAIRS // 2)
            pe.wait_ge(s_logits, 4 * PAIRS)
            out_part(3, range(0, 4))
            out_part(4, range(0, 4))
            pe.wait_ge(s_lo, UNITS + 4)
            pe.wait_ge(s_ylo, PAIRS)
            for g, first in enumerate((6, 6, 4, 4, 4)):
                out_part(g, range(first, PAIRS)).then_inc(s_group, 1)


def kernel(**inputs):
    import numpy as np
    import concourse.bacc as bacc
    from concourse.bass_utils import run_bass_kernel_spmd

    x = np.asarray(inputs["x"])[0]
    w_in = np.asarray(inputs["w_in"])[0]
    group = HEADS * HEAD_DIM
    names = ["qa", "ka", "va", "ga", "fa", "qb", "kb", "vb", "gb"]
    widths = [group] * 4 + [HEADS] + [group] * 4
    starts = np.cumsum([0] + widths)
    cols = {n: w_in[:, s:s + width] for n, s, width in zip(names, starts, widths)}

    def tiles(m):
        return m.reshape(KT, P, m.shape[1]).transpose(1, 0, 2)

    units = [tiles(m)[:, 2 * n:2 * n + 2].reshape(P, UNIT) for m in (cols["va"], cols["vb"]) for n in range(KT // 2)]

    def pair_unit(kind, p):
        m = cols[kind + ("a" if p < FOX_PAIRS else "b")]
        c = (p % FOX_PAIRS) * P
        return tiles(m[:, c:c + P]).reshape(P, UNIT)

    units += [pair_unit("g", p) for p in range(PAIRS)]
    for p in range(PAIRS):
        units += [pair_unit("q", p), pair_unit("k", p)]
    arrays = {
        "xt": tiles(x.T),
        "x": x.reshape(TT, P, D_MODEL).transpose(1, 0, 2),
        "g_pre": np.asarray(inputs["norm_pre_g"])[0].reshape(KT, P).T,
        "w_units": np.stack(units),
        "w_f": tiles(cols["fa"]),
        "f_bias": np.asarray(inputs["fox_forget_b"])[0].reshape(HEADS, 1),
        "w_out": np.asarray(inputs["w_out"])[0].reshape(PAIRS, P, D_MODEL),
        "g_post": np.asarray(inputs["norm_post_g"])[0].reshape(1, D_MODEL),
    }
    arrays = {n: np.ascontiguousarray(a) for n, a in arrays.items()}
    nc = bacc.Bacc("TRN2", target_bir_lowering=False, num_devices=1)
    aps = {n: nc.dram_tensor("in_" + n, a.shape, mybir.dt.from_np(a.dtype), kind="ExternalInput").ap()
           for n, a in arrays.items()}
    aps["out"] = nc.dram_tensor("out_0", (TT, P, D_MODEL), F32, kind="ExternalOutput").ap()
    hybrid_layer(nc, **aps)
    result = run_bass_kernel_spmd(nc, [{"in_" + n: a for n, a in arrays.items()}], core_ids=[0])
    return result.results[0]["out_0"].reshape(1, SEQ, D_MODEL)
```
